# Optimizing a Trainium2 kernel written in Bass

```python
import math
import jax, jax.numpy as jnp
from jax import lax
import numpy as np

D_MODEL = 2048
BATCH = 1
SEQ = 256
DEPTH = 1

SSM_EXPAND = 2
SSM_D_INNER = SSM_EXPAND * D_MODEL
SSM_HEAD_DIM = 64
SSM_HEADS = SSM_D_INNER // SSM_HEAD_DIM
SSM_GROUPS = 8
SSM_HEADS_PER_GROUP = SSM_HEADS // SSM_GROUPS
SSM_STATE = 128
SSM_CONV = 4
SSM_CHUNK = 256
SSM_CONV_CH = SSM_D_INNER + 2 * SSM_GROUPS * SSM_STATE

ATT_HEAD_DIM = 64
ATT_HEADS = D_MODEL // (2 * ATT_HEAD_DIM)
ATT_QK = 2 * ATT_HEADS * ATT_HEAD_DIM
ATT_V = ATT_HEADS * 2 * ATT_HEAD_DIM
Q_BLOCK = 128
ROPE_THETA = 10000.0

FFN_HIDDEN = (((8 * D_MODEL + 2) // 3 + 255) // 256) * 256

IN_SIZES = (SSM_D_INNER, SSM_CONV_CH, SSM_HEADS, ATT_QK, ATT_QK, ATT_V, D_MODEL, D_MODEL)
IN_TOTAL = sum(IN_SIZES)

NORM_EPS = 1e-6
SUBLN_EPS = 1e-5

kernel_name = "hybrid_gated_ssd_diffattn_swiglu"

def _in_splits():
    out, acc = [], 0
    for n in IN_SIZES[:-1]:
        acc += n
        out.append(acc)
    return out

def rms_norm(x, w, eps):
    xf = x.astype(jnp.float32)
    y = xf * lax.rsqrt(jnp.mean(xf * xf, axis=-1, keepdims=True) + eps)
    return (y * w.astype(jnp.float32)).astype(x.dtype)

def rotary(x, positions):
    half = x.shape[-1] // 2
    inv_freq = ROPE_THETA ** (-jnp.arange(half, dtype=jnp.float32) / half)
    ang = positions.astype(jnp.float32)[:, None] * inv_freq[None, :]
    cos = jnp.cos(ang)[None, :, None, :]
    sin = jnp.sin(ang)[None, :, None, :]
    xf = x.astype(jnp.float32)
    x1, x2 = xf[..., :half], xf[..., half:]
    return jnp.concatenate([x1 * cos - x2 * sin, x2 * cos + x1 * sin], axis=-1).astype(x.dtype)

def causal_depthwise_conv(u, w, b):
    k = w.shape[0]
    out = lax.conv_general_dilated(
        u, w[:, None, :].astype(u.dtype), window_strides=(1,), padding=[(k - 1, 0)],
        dimension_numbers=('NWC', 'WIO', 'NWC'), feature_group_count=u.shape[-1])
    return out + b.astype(u.dtype)

def ssd_chunked(xs, dt, A, Bm, Cm):
    b, s, g, r, p = xs.shape
    n = Bm.shape[-1]
    l = SSM_CHUNK
    pad = (-s) % l
    xdt = xs.astype(jnp.float32) * dt[..., None]
    dA = dt * A
    Bf = Bm.astype(jnp.float32)
    Cf = Cm.astype(jnp.float32)
    if pad:
        xdt = jnp.pad(xdt, ((0, 0), (0, pad), (0, 0), (0, 0), (0, 0)))
        dA = jnp.pad(dA, ((0, 0), (0, pad), (0, 0), (0, 0)))
        Bf = jnp.pad(Bf, ((0, 0), (0, pad), (0, 0), (0, 0)))
        Cf = jnp.pad(Cf, ((0, 0), (0, pad), (0, 0), (0, 0)))
    c = (s + pad) // l
    xdt = xdt.reshape(b, c, l, g, r, p)
    Bc = Bf.reshape(b, c, l, g, n)
    Cc = Cf.reshape(b, c, l, g, n)
    a_cs = jnp.cumsum(jnp.transpose(dA.reshape(b, c, l, g, r), (0, 3, 4, 1, 2)), axis=-1)

    causal = jnp.tril(jnp.ones((l, l), dtype=bool))
    decay_in = jnp.exp(jnp.where(causal, a_cs[..., :, None] - a_cs[..., None, :], -jnp.inf))
    cb = jnp.einsum('bclgn,bcsgn->bgcls', Cc, Bc)
    y_diag = jnp.einsum('bgrcls,bcsgrp->bclgrp', cb[:, :, None] * decay_in, xdt)

    decay_to_end = jnp.transpose(jnp.exp(a_cs[..., -1:] - a_cs), (0, 3, 4, 1, 2))
    states = jnp.einsum('bclgn,bclgrp->bcgrpn', Bc, xdt * decay_to_end[..., None])

    a_tot = jnp.pad(a_cs[..., -1], ((0, 0), (0, 0), (0, 0), (1, 0)))
    t_cs = jnp.cumsum(a_tot, axis=-1)
    chunk_causal = jnp.tril(jnp.ones((c + 1, c + 1), dtype=bool))
    decay_chunk = jnp.exp(jnp.where(chunk_causal, t_cs[..., :, None] - t_cs[..., None, :], -jnp.inf))
    states = jnp.concatenate([jnp.zeros_like(states[:, :1]), states], axis=1)
    states_in = jnp.einsum('bgrzc,bcgrpn->bzgrpn', decay_chunk, states)[:, :-1]

    decay_from_start = jnp.transpose(jnp.exp(a_cs), (0, 3, 4, 1, 2))
    y_off = jnp.einsum('bclgn,bcgrpn->bclgrp', Cc, states_in) * decay_from_start[..., None]

    y = (y_diag + y_off).reshape(b, c * l, g, r, p)
    return y[:, :s]

def mamba2_branch(z, xbc, dt_raw, conv_w, conv_b, dt_bias, a_log, d_skip, norm_w):
    b, s, _ = z.shape
    G, R, P, N = SSM_GROUPS, SSM_HEADS_PER_GROUP, SSM_HEAD_DIM, SSM_STATE
    xbc = jax.nn.silu(causal_depthwise_conv(xbc, conv_w, conv_b))
    xs, Bm, Cm = jnp.split(xbc, [SSM_D_INNER, SSM_D_INNER + G * N], axis=-1)
    xs = xs.reshape(b, s, G, R, P)
    Bm = Bm.reshape(b, s, G, N)
    Cm = Cm.reshape(b, s, G, N)
    dt = jax.nn.softplus(dt_raw.astype(jnp.float32) + dt_bias.astype(jnp.float32)).reshape(b, s, G, R)
    A = -jnp.exp(a_log.astype(jnp.float32)).reshape(G, R)
    y = ssd_chunked(xs, dt, A, Bm, Cm)
    y = y + d_skip.astype(jnp.float32).reshape(G, R)[..., None] * xs.astype(jnp.float32)
    y = y.reshape(b, s, SSM_D_INNER) * jax.nn.silu(z.astype(jnp.float32))
    y = y.reshape(b, s, G, SSM_D_INNER // G)
    y = y * lax.rsqrt(jnp.mean(y * y, axis=-1, keepdims=True) + SUBLN_EPS)
    y = y.reshape(b, s, SSM_D_INNER) * norm_w.astype(jnp.float32)
    return y.astype(z.dtype)

def diff_attention(q, k, v, q_norm_w, k_norm_w, lq1, lk1, lq2, lk2, subln_w, lam_init):
    b, s, _ = q.shape
    H, Dh = ATT_HEADS, ATT_HEAD_DIM
    q = q.reshape(b, s, 2 * H, Dh)
    k = k.reshape(b, s, 2 * H, Dh)
    v = v.reshape(b, s, H, 2 * Dh).astype(jnp.float32)
    pos = jnp.arange(s, dtype=jnp.int32)
    q = rotary(rms_norm(q, q_norm_w, NORM_EPS), pos).astype(jnp.float32)
    k = rotary(rms_norm(k, k_norm_w, NORM_EPS), pos).astype(jnp.float32)
    f = lambda t: t.astype(jnp.float32)
    lam = jnp.exp(jnp.sum(f(lq1) * f(lk1))) - jnp.exp(jnp.sum(f(lq2) * f(lk2))) + lam_init
    scale = Dh ** -0.5
    outs = []
    for i in range(s // Q_BLOCK):
        q0 = i * Q_BLOCK
        kv = q0 + Q_BLOCK
        sc = jnp.einsum('bqhd,bkhd->bhqk', q[:, q0:kv], k[:, :kv]) * scale
        mask = jnp.arange(kv)[None, :] <= (q0 + jnp.arange(Q_BLOCK))[:, None]
        sc = jnp.where(mask, sc, -jnp.inf)
        pr = jax.nn.softmax(sc, axis=-1).reshape(b, H, 2, Q_BLOCK, kv)
        wts = pr[:, :, 0] - lam * pr[:, :, 1]
        outs.append(jnp.einsum('bhqk,bkhe->bqhe', wts, v[:, :kv]))
    o = jnp.concatenate(outs, axis=1)
    o = rms_norm(o, subln_w, SUBLN_EPS) * (1.0 - lam_init)
    return o.reshape(b, s, ATT_V).astype(q.dtype)

def setup_inputs(seed: int = 0) -> dict:
    key = jax.random.key(seed)
    ks = jax.random.split(key, 24)
    f32 = jnp.float32
    L = DEPTH

    def normal(k, shape, scale):
        return jax.random.normal(k, shape, f32) * scale

    dt0 = jnp.exp(jax.random.uniform(ks[5], (L, SSM_HEADS), f32, math.log(1e-3), math.log(1e-1)))
    return {
        'x': normal(ks[0], (BATCH, SEQ, D_MODEL), 1.0),
        'mix_norm_w': 1.0 + normal(ks[1], (L, D_MODEL), 0.02),
        'w_in': normal(ks[2], (L, D_MODEL, IN_TOTAL), D_MODEL ** -0.5),
        'conv_w': normal(ks[3], (L, SSM_CONV, SSM_CONV_CH), SSM_CONV ** -0.5),
        'conv_b': normal(ks[4], (L, SSM_CONV_CH), 0.02),
        'dt_bias': dt0 + jnp.log(-jnp.expm1(-dt0)),
        'a_log': jnp.log(jax.random.uniform(ks[6], (L, SSM_HEADS), f32, 1.0, 16.0)),
        'd_skip': 1.0 + normal(ks[7], (L, SSM_HEADS), 0.02),
        'ssm_norm_w': 1.0 + normal(ks[8], (L, SSM_D_INNER), 0.02),
        'w_ssm_proj': normal(ks[9], (L, SSM_D_INNER, D_MODEL), SSM_D_INNER ** -0.5),
        'q_norm_w': 1.0 + normal(ks[10], (L, ATT_HEAD_DIM), 0.02),
        'k_norm_w': 1.0 + normal(ks[11], (L, ATT_HEAD_DIM), 0.02),
        'lambda_q1': normal(ks[12], (L, ATT_HEAD_DIM), 0.1),
        'lambda_k1': normal(ks[13], (L, ATT_HEAD_DIM), 0.1),
        'lambda_q2': normal(ks[14], (L, ATT_HEAD_DIM), 0.1),
        'lambda_k2': normal(ks[15], (L, ATT_HEAD_DIM), 0.1),
        'subln_w': 1.0 + normal(ks[16], (L, 2 * ATT_HEAD_DIM), 0.02),
        'w_attn_proj': normal(ks[17], (L, ATT_V, D_MODEL), ATT_V ** -0.5),
        'w_out': normal(ks[18], (L, D_MODEL, D_MODEL), D_MODEL ** -0.5),
        'ffn_norm_w': 1.0 + normal(ks[19], (L, D_MODEL), 0.02),
        'w_ffn_gate': normal(ks[20], (L, D_MODEL, FFN_HIDDEN), D_MODEL ** -0.5),
        'w_ffn_up': normal(ks[21], (L, D_MODEL, FFN_HIDDEN), D_MODEL ** -0.5),
        'w_ffn_down': normal(ks[22], (L, FFN_HIDDEN, D_MODEL), FFN_HIDDEN ** -0.5),
    }

def reference(x, mix_norm_w, w_in, conv_w, conv_b, dt_bias, a_log, d_skip, ssm_norm_w, w_ssm_proj,
              q_norm_w, k_norm_w, lambda_q1, lambda_k1, lambda_q2, lambda_k2, subln_w, w_attn_proj,
              w_out, ffn_norm_w, w_ffn_gate, w_ffn_up, w_ffn_down):
    splits = _in_splits()
    for layer in range(DEPTH):
        lam_init = 0.8 - 0.6 * math.exp(-0.3 * layer)
        h = rms_norm(x, mix_norm_w[layer], NORM_EPS)
        proj = jnp.einsum('bsd,dn->bsn', h, w_in[layer])
        z, xbc, dt_raw, q, k, v, g_ssm, g_att = jnp.split(proj, splits, axis=-1)
        y_ssm = mamba2_branch(z, xbc, dt_raw, conv_w[layer], conv_b[layer], dt_bias[layer],
                              a_log[layer], d_skip[layer], ssm_norm_w[layer])
        y_att = diff_attention(q, k, v, q_norm_w[layer], k_norm_w[layer], lambda_q1[layer],
                               lambda_k1[layer], lambda_q2[layer], lambda_k2[layer],
                               subln_w[layer], lam_init)
        b_ssm = jnp.einsum('bse,ed->bsd', y_ssm, w_ssm_proj[layer])
        b_att = jnp.einsum('bse,ed->bsd', y_att, w_attn_proj[layer])
        merged = jax.nn.sigmoid(g_ssm) * b_ssm + jax.nn.sigmoid(g_att) * b_att
        x = x + jnp.einsum('bsd,de->bse', merged, w_out[layer]).astype(x.dtype)
        h = rms_norm(x, ffn_norm_w[layer], NORM_EPS)
        a = jax.nn.silu(jnp.einsum('bsd,df->bsf', h, w_ffn_gate[layer])) * jnp.einsum('bsd,df->bsf', h, w_ffn_up[layer])
        x = x + jnp.einsum('bsf,fd->bsd', a, w_ffn_down[layer]).astype(x.dtype)
    return x


_drawn_inputs = setup_inputs


def setup_inputs(seed=0):
    import zlib

    import numpy as np

    out = dict(_drawn_inputs(seed))
    spreads = {}
    factors = {'conv_b': 4.219,
     'd_skip': 8.0,
     'ssm_norm_w': 5.824,
     'q_norm_w': 6.723,
     'k_norm_w': 7.165,
     'lambda_q2': 8.0,
     'subln_w': 7.018,
     'ffn_norm_w': 4.587}
    for name, (base, spread) in spreads.items():
        noise = np.random.default_rng([zlib.crc32(name.encode()), seed]).standard_normal(out[name].shape)
        drawn = base * np.exp(spread * noise) if base else spread * noise
        out[name] = __import__('jax').numpy.asarray(drawn.astype(out[name].dtype))
    for name, factor in factors.items():
        out[name] = (out[name] * factor).astype(out[name].dtype)
    return out
```

```python
from contextlib import ExitStack, contextmanager

import concourse.bass as bass
import numpy as np
from concourse import mybir

F32 = mybir.dt.float32
F32R = mybir.dt.float32r
BF16 = mybir.dt.bfloat16
ALU = mybir.AluOpType
ACT = mybir.ActivationFunctionType
AX = mybir.AxisListType.X

P = 128
T = 256
TT = T // P
D = 2048
KD = D // P
DI = 2 * D
KI = DI // P
HS = 64
HP = 64
G = 8
HG = HS // G
NS = 128
TAPS = 4
XBC = DI + 2 * G * NS
STARTED = 1
NA = 16
DH = 64
FF = 5632
KF = FF // P
CW = 512
CT = CW // P
UK = 2
RING = 4
LEAD = 4
UPC = KD // UK

COL_Z = 0
COL_X = DI
COL_BC = COL_X + DI
COL_DT = COL_X + XBC
COL_Q = COL_DT + HS
COL_K = COL_Q + D
COL_V = COL_K + D
COL_GS = COL_V + D
COL_GA = COL_GS + D

NORM_EPS = 1e-6
SUBLN_EPS = 1e-5
LAM_INIT = 0.8 - 0.6 * float(np.exp(-0.3 * 0))
MASKED = -1e30

C_ID, C_TRI, C_MASK_SL, C_MASK_QK, C_ROPE = 0, P, 2 * P, 3 * P, 4 * P
C_ALL = C_ROPE + TT * 2 * DH

R_CONV = 2 * (XBC // P)
R_BIAS, R_MIX, R_FFN, R_SSM, R_SUB = 0, 48, 64, 80, 112
R_ALL = 113


def constants():
    c = np.zeros((P, C_ALL), np.float32)
    c[:, C_ID:C_ID + P] = np.eye(P, dtype=np.float32)
    row, col = np.arange(P)[:, None], np.arange(P)[None, :]
    c[:, C_TRI:C_TRI + P] = (row <= col)
    c[:, C_MASK_SL:C_MASK_SL + P] = np.where(row <= col, 0.0, MASKED)
    c[:, C_MASK_QK:C_MASK_QK + P] = np.where(col <= row, 0.0, MASKED)
    half = DH // 2
    inv = np.float32(10000.0) ** (-np.arange(half, dtype=np.float32) / np.float32(half))
    angle = np.arange(T, dtype=np.float32)[:, None] * inv.astype(np.float32)[None, :]
    cos, sin = np.cos(angle).astype(np.float32), np.sin(angle).astype(np.float32)
    for t in range(TT):
        r = slice(t * P, (t + 1) * P)
        at = C_ROPE + t * 2 * DH
        c[:, at:at + 2 * DH] = np.concatenate([cos[r], cos[r], -sin[r], sin[r]], axis=1)
    return c


class Tally:

    def __init__(self):
        self.base, self.n = 0, 0

    def step(self, k=1):
        self.n += k
        return self.base + self.n

    def now(self, k=0):
        return self.base + self.n + k


@contextmanager
def repeat(engine, times, counts):
    before = [t.n for t, _ in counts]
    with engine.Fori(0, times) as i:
        for (t, per), n in zip(counts, before):
            t.base, t.n = i * per + n, 0
        yield i
        for t, per in counts:
            assert t.n == per, (t.n, per)
    for (t, per), n in zip(counts, before):
        t.base, t.n = 0, n + times * per


def layer(nc, x, mix_norm_w, w_in, conv_w, conv_b, dt_bias, a_log, d_skip, ssm_norm_w, w_ssm_proj,
          q_norm_w, k_norm_w, lambda_q1, lambda_k1, lambda_q2, lambda_k2, subln_w, w_attn_proj,
          w_out, ffn_norm_w, w_ffn_gate, w_ffn_up, w_ffn_down, consts, out):
    ctx = ExitStack()
    with ctx:
        base = -(-nc.sbuf_base // 64) * 64

        def at(name, kb, shape, dtype=F32):
            return nc.alloc_sbuf_tensor_at(name, shape, dtype, offset=base + int(kb * 1024))

        def sem(name):
            return ctx.enter_context(nc.semaphore(name))

        w_raw = at("w_raw", 0, [P, RING, UK, CW])
        w_hi = at("w_hi", 16, [P, RING, UK, CW], F32R)
        w_lo = at("w_lo", 32, [P, RING, UK, CW], F32R)
        h_hi = at("h_hi", 48, [P, KD, T], F32R)
        h_lo = at("h_lo", 64, [P, KD, T], F32R)
        x2T_hi = at("x2T_hi", 48, [P, KD, T], F32R)
        x2T_lo = at("x2T_lo", 64, [P, KD, T], F32R)
        cst = at("cst", 80, [P, 3 * P])
        ident, tri, mask_sl = (cst[:, a:a + P] for a in (C_ID, C_TRI, C_MASK_SL))
        ones = at("ones", 81.5, [P, P])
        ident_b = at("ident_b", 82, [P, P], BF16)
        mask_b = at("mask_b", 82.25, [P, P], BF16)
        taps = at("taps", 82.5, [P, TAPS, XBC // P])
        cols = at("cols", 83.25, [P, P])
        dt_bias_b = at("dt_bias_b", 83.75, [P, HS])
        decay_rate = at("decay_rate", 84, [P, HS])
        d_skip_b = at("d_skip_b", 84.25, [P, HS])
        dt = at("dt", 84.5, [P, TT, HS])
        dA = at("dA", 85, [P, TT, HS])
        neg_acs = at("neg_acs", 85.5, [P, TT, HS])
        small = at("small", 86, [P, 128])
        pool_constants = at("pool_constants", 86.5, [P, 6, 16])
        qk = at("qk", 87, [P, 2, NA, TT, P])
        ya_hi = at("ya_hi", 87, [P, KD, T], F32R)
        ya_lo = at("ya_lo", 103, [P, KD, T], F32R)
        v_all = at("v_all", 119, [P, TT, D])
        bc = at("bc", 135, [P, 2 * G, T])
        merge_a = at("merge_a", 151, [P, KD, T])
        sq = at("sq", 167, [P, TT, CW])
        rot_a = at("rot_a", 171, [P, TT, CW])
        rot_b = at("rot_b", 175, [P, TT, CW])
        rope = at("rope", 179, [P, 2, TT, 2, DH])
        qk_row = at("qk_row", 181, [P, 2, 2, TT, P])
        qkT = at("qkT", 185, [P, 2, T])
        prob = at("prob", 187, [P, 2, 3 * P])
        wts = at("wts", 190, [P, 3 * P])
        wtsT = at("wtsT", 191.5, [P, 3 * P])
        o_row = at("o_row", 193, [P, TT, P])
        conv_a = at("conv_a", 194, [P, CT, T])
        o_sq = at("o_sq", 198, [P, TT, P])
        att = at("att", 199, [P, 64])
        rows = at("rows", 200, [P, 3, P])
        bcast = at("bcast", 202, [P, 9, HS])
        x_row = at("x_row", 119, [P, TT, D])
        rope_in = at("rope_in", 205, [P, TT, 2, DH])
        mask_in = at("mask_in", 206, [P, P])
        yT = at("yT", 87, [P, KI, T])
        y_lo = at("y_lo", 87, [P, KI, T], F32R)
        y_hi = at("y_hi", 119, [P, KI, T], F32R)
        wdt = at("wdt", 119, [P, KD, HS])
        wdt_hi = at("wdt_hi", 123, [P, KD, HS], F32R)
        wdt_lo = at("wdt_lo", 127, [P, KD, HS], F32R)
        decay = at("decay", 167, [P, HG, 3 * P])
        acs_b = at("acs_b", 179, [P, 2, HG // 2, T])
        acs_m = at("acs_m", 187, [P, 2, HG // 2, P])
        conv_x = at("conv_x", 191, [P, CT, T])
        y_row = at("y_row", 195, [P, TT, CW])
        xdt = at("xdt", 199, [P, TT, CW])
        z_row = at("z_row", 203, [P, TT, CW])
        bT = at("bT", 131, [P, T])
        cb = at("cb", 132, [P, 3 * P])
        acsT = at("acsT", 133.5, [HS, T])
        soft = at("soft", 167, [P, 6, TT * HS])
        gate_s = at("gate_s", 167, [P, KD, T])
        m_hi = at("m_hi", 151, [P, KD, T], F32R)
        m_lo = at("m_lo", 167, [P, KD, T], F32R)
        m_row = at("m_row", 199, [P, CT, T])
        x2 = at("x2", 183, [P, TT, D])
        a_hi = at("a_hi", 87, [P, KF, T], F32R)
        a_lo = at("a_lo", 131, [P, KF, T], F32R)
        gate_f = at("gate_f", 175, [P, CT, T])
        up_f = at("up_f", 179, [P, CT, T])
        rstd_b = at("rstd_b", 203, [P, T])
        x2_sq = at("x2_sq", 87, [P, TT, D])
        diag = at("diag", 204, [P, TT, P])
        out_row = at("out_row", 175, [P, 2, TT, CW])

        acs_dram = nc.dram_tensor("acs_scratch", (HS, T), F32, kind="Internal").ap()

        acc = [ctx.enter_context(nc.psum_tensor(f"acc{p}", [P, 2, CW], F32)) for p in range(2)]
        side = ctx.enter_context(nc.psum_tensor("side", [P, 4, CW], F32))

        raw_in = [sem(f"raw_in{r}") for r in range(RING)]
        hi_ready = sem("hi_ready")
        lo_ready = sem("lo_ready")
        mm_done = sem("mm_done")
        acc_free = [sem(f"acc_free{p}") for p in range(2)]
        const_in, rows_in, bcast_in = sem("const_in"), sem("rows_in"), sem("bcast_in")
        x_in = [sem(f"x_in{t}") for t in range(TT)]
        act_step, dve_step, pool_step = sem("act_step"), sem("dve_step"), sem("pool_step")
        ss_ready, rstd_ready = sem("ss_ready"), sem("rstd_ready")
        x_normed, side_T, side_hi, side_lo = sem("x_normed"), sem("side_T"), sem("side_hi"), sem("side_lo")
        rows_T, cols_ready, setup_done = sem("rows_T"), sem("cols_ready"), sem("setup_done")
        eps_ready = sem("eps_ready")
        lam_sums, lam_exps = sem("lam_sums"), sem("lam_exps")
        conv_first, conv_done = sem("conv_first"), sem("conv_done")
        sq_read = sem("sq_read")
        v_copied = sem("v_copied")
        bc_ready = sem("bc_ready")
        gate_a_ready, merged_a = sem("gate_a_ready"), sem("merged_a")
        row_in = [sem(f"row_in{a}") for a in range(2)]
        qk_T, qkT_ready, scores, max_ready = sem("qk_T"), sem("qkT_ready"), sem("scores"), sem("max_ready")
        prob_ready, wts_ready, wts_T, wtsT_ready = sem("prob_ready"), sem("wts_ready"), sem("wts_T"), sem("wtsT_ready")
        pv, o_sums, o_rstd, o_ready, o_T = sem("pv"), sem("o_sums"), sem("o_rstd"), sem("o_ready"), sem("o_T")
        ya_hi_ready, ya_lo_ready, qk_ready = sem("ya_hi_ready"), sem("ya_lo_ready"), sem("qk_ready")
        wdt_in, wdt_hi_ready, wdt_ready, dt_sum, dt_u, dt_exp = (sem(n) for n in (
            "wdt_in", "wdt_hi_ready", "wdt_ready", "dt_sum", "dt_u", "dt_exp"))
        dA_ready, acs_sum, acs_ready, acs_out = sem("dA_ready"), sem("acs_sum"), sem("acs_ready"), sem("acs_out")
        acs_in = [sem(f"acs_in{h}") for h in range(2)]
        acs_masked, decay_exp, decay_ready = sem("acs_masked"), sem("decay_exp"), sem("decay_ready")
        bT_ready, cb_sum, cb_ready = sem("bT_ready"), sem("cb_sum"), sem("cb_ready")
        xs_ready, xs_T, xdt_ready, xrow_ready, skip_ready = (sem(n) for n in (
            "xs_ready", "xs_T", "xdt_ready", "xrow_ready", "skip_ready"))
        z_ready, y_sum, y_gated, y_squared, y_rstd, y_ready, y_T, yT_ready = (sem(n) for n in (
            "z_ready", "y_sum", "y_gated", "y_squared", "y_rstd", "y_ready", "y_T", "yT_ready"))
        y_hi_ready, y_lo_ready, y_added = sem("y_hi_ready"), sem("y_lo_ready"), sem("y_added")
        m_ready, m_hi_ready, m_lo_ready = sem("m_ready"), sem("m_hi_ready"), sem("m_lo_ready")
        x2_in, x2_ready, x2_T, x2_hi_ready, x2_lo_ready = (sem(n) for n in (
            "x2_in", "x2_ready", "x2_T", "x2_hi_ready", "x2_lo_ready"))
        x2_ss, x2_rstd, diag_ready, rstd_T, rstd_b_ready = (sem(n) for n in (
            "x2_ss", "x2_rstd", "diag_ready", "rstd_T", "rstd_b_ready"))
        gate_f_scaled, gate_f_ready, a_ready, a_hi_ready, a_lo_ready = (sem(n) for n in (
            "gate_f_scaled", "gate_f_ready", "a_ready", "a_hi_ready", "a_lo_ready"))
        out_ready, out_done = sem("out_ready"), [sem(f"out_done{p}") for p in range(2)]

        block = ctx.enter_context(nc.Block())

        conv_rows = conv_w[0].rearrange("j (m p) -> (j m) p", p=P)

        @block.sync
        def _(sp):
            unit = Tally()

            def load(source, row_tile, col):
                s = unit.n
                if not (unit.n < RING and isinstance(unit.base, int)):
                    sp.wait_ge(lo_ready, unit.now(1 - RING))
                src = source[0, row_tile * P:(row_tile + UK) * P, bass.ds(col, CW)]
                sp.dma_start(w_raw[:, s % RING], src.rearrange("(k p) n -> p k n", p=P)).then_inc(raw_in[s % RING], 16)
                unit.step()

            def chunk(source, col, units=UPC):
                for u in range(units):
                    load(source, u * UK, col)

            for c in range(4):
                chunk(w_in, COL_Q + c * CW)
            for first, pairs in ((COL_K, 2), (COL_V, 2)):
                with repeat(sp, pairs, [(unit, 2 * UPC)]) as i:
                    for c in range(2):
                        chunk(w_in, i * (2 * CW) + first + c * CW)
            sp.wait_ge(qk_ready, 2 * D // CW)
            for n, first in enumerate((COL_BC, COL_GA)):
                with repeat(sp, 2, [(unit, 2 * UPC)]) as i:
                    for c in range(2):
                        for u in range(UPC):
                            if u in (4, 5):
                                a = u - 4
                                head = 8 * n + 2 * c + a
                                sp.wait_ge(qk_T, i * 4 + max(head - 1, 0) + STARTED)
                                src = qk[:, :, bass.ds(i * 4 + head, 1)].rearrange("p w o t d -> p w (o t) d")
                                sp.dma_start(qk_row[:, a], src).then_inc(row_in[a], 16)
                            load(w_in, u * UK, i * (2 * CW) + first + c * CW)
            with repeat(sp, 2, [(unit, 2 * UPC)]) as i:
                for c in range(2):
                    chunk(w_attn_proj, i * (2 * CW) + c * CW)
            sp.wait_ge(pv, NA + STARTED)
            sp.dma_start(wdt[:], w_in[0, :, COL_DT:COL_DT + HS].rearrange("(k p) n -> p k n", p=P)).then_inc(wdt_in, 16)

            with repeat(sp, G, [(unit, 2 * UPC)]) as i:
                chunk(w_in, i * CW + COL_X)
                chunk(w_in, (i + i) * (CW // 2) + COL_Z)
            with repeat(sp, 2, [(unit, 2 * UPC)]) as i:
                for c in range(2):
                    chunk(w_in, i * (2 * CW) + COL_GS + c * CW)
            sp.wait_ge(y_T, G)
            sp.dma_start(x2[:], x[0].rearrange("(t p) d -> p t d", p=P)).then_inc(x2_in, 16)
            with repeat(sp, 2, [(unit, 4 * UPC)]) as i:
                for c in range(2):
                    chunk(w_ssm_proj, i * (2 * CW) + c * CW, 2 * UPC)
            with repeat(sp, 2, [(unit, 2 * UPC)]) as i:
                for c in range(2):
                    chunk(w_out, i * (2 * CW) + c * CW)
            with repeat(sp, FF // CW, [(unit, 2 * UPC)]) as i:
                chunk(w_ffn_gate, i * CW)
                chunk(w_ffn_up, i * CW)
            out_v = out[0].rearrange("(t p) d -> p t d", p=P)

            def store(c):
                sp.wait_ge(out_ready, c + 1)
                sp.dma_start(out_v[:, :, c * CW:(c + 1) * CW], out_row[:, c % 2]).then_inc(out_done[c % 2], 16)

            for c in range(D // CW):
                for u in range(KF // UK):
                    load(w_ffn_down, u * UK, c * CW)
                    if c and u == KF // UK // 2:
                        store(c - 1)
            store(D // CW - 1)
            for p in range(2):
                sp.wait_ge(out_done[p], 16 * D // CW // 2)

        @block.scalar
        def _(act):
            unit, own = Tally(), Tally()
            nc.scalar.dma_start(cst[:], consts[:, :3 * P]).then_inc(const_in, 16)
            nc.scalar.dma_start(mask_in[:], consts[:, C_MASK_QK:C_MASK_QK + P]).then_inc(const_in, 16)
            nc.scalar.dma_start(rope_in[:], consts[:, C_ROPE:].rearrange("p (t w d) -> p t w d", t=TT, w=2)).then_inc(const_in, 16)
            for t in range(TT):
                nc.scalar.dma_start(x_row[:, t], x[0, t * P:(t + 1) * P, :]).then_inc(x_in[t], 16)
            for j in range(2):
                nc.scalar.dma_start(rows[0:R_CONV, j], conv_rows[j * R_CONV:(j + 1) * R_CONV, :]).then_inc(rows_in, 16)
            for first, last, vector in ((R_BIAS, R_MIX, conv_b), (R_MIX, R_FFN, mix_norm_w), (R_FFN, R_SSM, ffn_norm_w),
                                        (R_SSM, R_SUB, ssm_norm_w), (R_SUB, R_ALL, subln_w)):
                nc.scalar.dma_start(rows[first:last, 2], vector[0].rearrange("(m p) -> m p", p=P)).then_inc(rows_in, 16)
            for n, vector in enumerate((dt_bias, a_log, d_skip, q_norm_w, k_norm_w, lambda_q1, lambda_k1, lambda_q2, lambda_k2)):
                nc.scalar.dma_start(bcast[:, n], vector[0].partition_broadcast(P)).then_inc(bcast_in, 16)
            for stage in (qk_T, scores, prob_ready, wts_ready, wts_T, pv, o_sums, o_T, ya_lo_ready):
                nc.scalar.sem_inc(stage, STARTED)
            nc.scalar.sem_inc(acc_free[0], 1)
            nc.scalar.sem_inc(acc_free[1], 1)

            def link(instruction):
                instruction.then_inc(act_step, 1)
                act.wait_ge(act_step, own.step())

            def split_hi():
                s, r = unit.n, unit.n % RING
                act.wait_ge(raw_in[r], unit.base * (16 // RING) + 16 * (s // RING + 1))
                if not (isinstance(unit.base, int) and s < RING):
                    act.wait_ge(mm_done, unit.now(1 - RING))
                nc.scalar.activation(w_hi[:, r], w_raw[:, r], ACT.Copy).then_inc(hi_ready, 1)
                unit.step()

            def chunk_done():
                act.wait_ge(mm_done, unit.now(-LEAD))

            def sums(p):
                return acc[p][:].rearrange("p b (n t) -> p (b n) t", t=T)

            for t in range(TT):
                act.wait_ge(x_in[t], 16)
                nc.scalar.activation(qk[:, 0, 8 * t:8 * t + 8], x_row[:, t].rearrange("p (a b c) -> p a b c", a=8, b=2),
                                     ACT.Square, accum_out=small[:, t:t + 1]).then_inc(ss_ready, 1)
            act.wait_ge(rows_T, 1)
            nc.scalar.activation(taps[:].rearrange("p j m -> p (j m)"), side[:, 0, 0:2 * R_CONV], ACT.Copy).then_inc(cols_ready, 1)
            nc.scalar.activation(cols[:, 0:R_ALL], side[:, 0, 2 * R_CONV:2 * R_CONV + R_ALL], ACT.Copy).then_inc(cols_ready, 1)
            act.wait_ge(cols_ready, 2)
            act.wait_ge(bcast_in, 9 * 16)
            nc.scalar.activation(decay_rate[:], bcast[:, 1], ACT.Exp).then_inc(lam_exps, 1)
            act.wait_ge(lam_sums, 2)
            nc.scalar.activation(small[:, 83:85], small[:, 81:83], ACT.Exp).then_inc(lam_exps, 1)
            for b in range(KD // 2):
                act.wait_ge(side_T, b + 1)
                for k in (2 * b, 2 * b + 1):
                    last = nc.scalar.activation(h_hi[:, k], side[:, b % 4, (k % 2) * T:(k % 2 + 1) * T], ACT.Copy,
                                                scale=cols[:, R_MIX + k:R_MIX + k + 1])
                last.then_inc(side_hi, 1)

            for _ in range(LEAD):
                split_hi()

            for which in range(2):
                with repeat(act, 2, [(unit, 2 * UPC)]) as i:
                    for c in range(2):
                        for u in range(UPC):
                            split_hi()
                        chunk_done()
                        nc.scalar.activation(sq[:], acc[c][:], ACT.Square).then_inc(sq_read, 1)
            with repeat(act, 2, [(unit, 2 * UPC)]) as i:
                for c in range(2):
                    for u in range(UPC):
                        split_hi()
                    chunk_done()
                    nc.scalar.activation(v_all[:, :, bass.ds(i * (2 * CW) + c * CW, CW)], acc[c][:], ACT.Copy).then_inc(acc_free[c], 1)

            def conv_first_taps(c, tile, buf):
                chunk_done()
                for n in range(CT):
                    last = nc.scalar.activation(buf[:, n], sums(c)[:, n], ACT.Identity,
                                                bias=cols[:, bass.ds(tile + (R_BIAS + n), 1)],
                                                scale=taps[:, TAPS - 1, bass.ds(tile + n, 1)])
                    if n % 2:
                        last.then_inc(conv_first, 1)

            def qk_transposed(h):
                act.wait_ge(qk_T, h + 1 + STARTED)
                act.wait_ge(scores, h + STARTED)
                nc.scalar.activation(qkT[:].rearrange("p w t -> p (w t)"), side[:, 0, :], ACT.Copy).then_inc(qkT_ready, 1)

            def head_exps(h, b):
                act.wait_ge(max_ready, h + 1)
                act.wait_ge(wts_ready, h + STARTED)
                for q in range(TT):
                    cut = slice(0, P) if q == 0 else slice(P, 3 * P)
                    for m in range(2):
                        n = 32 * b + 2 * q + m
                        last = nc.scalar.activation(prob[:, m, cut], side[:, 1 + m, cut], ACT.Exp, bias=att[:, n:n + 1],
                                                    accum_out=att[:, n + 4:n + 5])
                last.then_inc(prob_ready, 1)

            def weights_transposed(h):
                act.wait_ge(wts_T, h + 1 + STARTED)
                act.wait_ge(pv, h + STARTED)
                nc.scalar.activation(wtsT[:], side[:, 0, 0:3 * P], ACT.Copy).then_inc(wtsT_ready, 1)

            def output_hi(h):
                act.wait_ge(o_T, h + 1 + STARTED)
                nc.scalar.activation(ya_hi[:, bass.ds(h, 1)].rearrange("p o t -> p (o t)"), side[:, 0, 0:T], ACT.Copy,
                                     scale=small[:, 96:97]).then_inc(ya_hi_ready, 1)

            def chunk_with_heads(a):
                for u in range(UPC):
                    split_hi()
                    if u == 0:
                        qk_transposed(a)
                    if u == 1:
                        head_exps(a, 0)
                    if u == 2:
                        qk_transposed(a + 1)
                    if u == 3:
                        weights_transposed(a)
                        head_exps(a + 1, 1)
                    if u == 5:
                        weights_transposed(a + 1)
                    if u >= 6:
                        output_hi(a + (u - 6))

            with repeat(act, 2, [(unit, 2 * UPC)]) as i:
                for c in range(2):
                    chunk_with_heads(i * 4 + 2 * c)
                    conv_first_taps(c, i * (2 * CT) + (DI // P + c * CT), conv_a)
                    act.wait_ge(conv_done, i * 2 + c + 1)
                    nc.scalar.activation(bc[:, bass.ds(i * (2 * CT) + c * CT, CT)], conv_a[:], ACT.Silu).then_inc(bc_ready, 1)
            with repeat(act, 2, [(unit, 2 * UPC)]) as i:
                for c in range(2):
                    chunk_with_heads(i * 4 + (8 + 2 * c))
                    chunk_done()
                    nc.scalar.activation(merge_a[:, bass.ds(i * (2 * CT) + c * CT, CT)], sums(c), ACT.Sigmoid).then_inc(acc_free[c], 1)
            with repeat(act, 2, [(unit, 2 * UPC)]) as i:
                for c in range(2):
                    for u in range(UPC):
                        split_hi()

            def tail_squares(g):
                act.wait_ge(y_gated, g + 1)
                for t in range(TT):
                    last = nc.scalar.activation(z_row[:, t], y_row[:, t], ACT.Square, accum_out=small[:, 4 + t:5 + t])
                last.then_inc(y_squared, 1)

            def x_chunk(g, head):
                for u in range(UPC):
                    split_hi()
                    if head:
                        if u == 0:
                            act.wait_ge(wdt_in, 16)
                            nc.scalar.activation(wdt_hi[:], wdt[:], ACT.Copy).then_inc(wdt_hi_ready, 1)
                        if u == 4:
                            act.wait_ge(dt_u, 1)
                            nc.scalar.activation(soft[:, 2], soft[:, 1], ACT.Exp).then_inc(dt_exp, 1)
                        if u == 7:
                            act.wait_ge(acs_sum, 1)
                            nc.scalar.activation(neg_acs[:].rearrange("p t h -> p (t h)"), side[:, 1, 0:TT * HS], ACT.Copy,
                                                 scale=-1.0).then_inc(acs_ready, 1)
                            nc.scalar.activation(acsT[:], side[0:HS, 2, 0:T], ACT.Copy).then_inc(acs_ready, 1)
                            act.wait_ge(acs_ready, 2)
                    elif u == 3:
                        tail_squares(g - 1)
                    if u == 6:
                        act.wait_ge(cb_sum, g)
                        nc.scalar.activation(bT[:], bc[:, bass.ds(g, 1)].rearrange("p o t -> p (o t)"), ACT.Copy).then_inc(bT_ready, 1)
                conv_first_taps(0, g * CT, conv_x)

            def exps(g, hf):
                act.wait_ge(acs_masked, (g * 2 + hf + 1) * 2)
                if hf == 0:
                    act.wait_ge(y_sum, g)
                for h4 in range(HG // 2):
                    h = hf * (HG // 2) + h4
                    nc.scalar.activation(decay[:, h, 0:T], acs_b[:, hf, h4], ACT.Exp, bias=neg_acs[:, 0, bass.ds(g * HG + h, 1)])
                    last = nc.scalar.activation(decay[:, h, T:T + P], acs_m[:, hf, h4], ACT.Exp,
                                                bias=neg_acs[:, 1, bass.ds(g * HG + h, 1)])
                last.then_inc(decay_exp, 1)

            def z_chunk(g):
                for u in range(UPC):
                    split_hi()
                    if u == 0:
                        act.wait_ge(conv_done, g + 5)
                        nc.scalar.activation(conv_x[:], conv_x[:], ACT.Silu).then_inc(xs_ready, 1)
                    if u == 1:
                        act.wait_ge(cb_sum, g + 1)
                        nc.scalar.activation(cb[:], side[:, 0, 0:3 * P], ACT.Copy).then_inc(cb_ready, 1)
                    if u == 2:
                        exps(g, 0)
                    if u == 3:
                        act.wait_ge(xdt_ready, g + 1)
                        nc.scalar.activation(y_row[:], side[:, 2:4], ACT.Copy).then_inc(xrow_ready, 1)
                    if u == 4:
                        exps(g, 1)
                chunk_done()
                nc.scalar.activation(z_row[:], acc[1][:], ACT.Silu).then_inc(z_ready, 1)
                act.wait_ge(z_ready, g + 1)
                nc.scalar.sem_inc(acc_free[1], 1)

            x_chunk(0, True)
            z_chunk(0)
            with repeat(act, G - 1, [(unit, 2 * UPC)]) as i:
                x_chunk(i + 1, False)
                z_chunk(i + 1)

            for c in range(4):
                for u in range(UPC):
                    split_hi()
                    if c == 0 and u == 3:
                        tail_squares(G - 1)
                    if c >= 1 and u in (1, 3, 5):
                        n = 3 * (c - 1) + (u - 1) // 2
                        if n < KI // 4:
                            act.wait_ge(yT_ready, G)
                            nc.scalar.activation(y_hi[:, 4 * n:4 * n + 4], yT[:, 4 * n:4 * n + 4], ACT.Copy).then_inc(y_hi_ready, 1)
                chunk_done()
                nc.scalar.activation(gate_s[:, c * CT:(c + 1) * CT], sums(c % 2), ACT.Sigmoid).then_inc(acc_free[c % 2], 1)

            with repeat(act, 2, [(unit, 4 * UPC)]) as i:
                for c in range(2):
                    for u in range(2 * UPC):
                        split_hi()
                    act.wait_ge(m_ready, i * 2 + c + 1)
                    nc.scalar.activation(m_hi[:, bass.ds(i * (2 * CT) + c * CT, CT)], m_row[:], ACT.Copy).then_inc(m_hi_ready, 1)

            def residual_hi(c):
                act.wait_ge(x2_T, c + 1)
                for n in range(CT):
                    k = c * CT + n
                    last = nc.scalar.activation(x2T_hi[:, k], side[:, 2:4].rearrange("p b (n t) -> p (b n) t", t=T)[:, n],
                                                ACT.Copy, scale=cols[:, R_FFN + k:R_FFN + k + 1])
                last.then_inc(x2_hi_ready, 1)

            for c in range(4):
                for u in range(UPC):
                    split_hi()
                    if c and u == 3:
                        residual_hi(c - 1)

            def gate_silu(i):
                act.wait_ge(gate_f_scaled, i + 1)
                nc.scalar.activation(gate_f[:], gate_f[:], ACT.Silu).then_inc(gate_f_ready, 1)

            def up_hi(i):
                act.wait_ge(a_ready, i + 1)
                nc.scalar.activation(a_hi[:, bass.ds(i * CT, CT)], up_f[:], ACT.Copy).then_inc(a_hi_ready, 1)

            def ffn_pair(i, head):
                for u in range(UPC):
                    split_hi()
                    if head and u == 2:
                        residual_hi(3)
                    if head and u == 3:
                        for t in range(TT):
                            last = nc.scalar.activation(x2_sq[:, t], x2[:, t], ACT.Square, accum_out=small[:, 86 + t:87 + t])
                        last.then_inc(x2_ss, 1)
                    if head and u == 6:
                        act.wait_ge(rstd_T, 1)
                        nc.scalar.activation(rstd_b[:], side[:, 0, 0:T], ACT.Copy).then_inc(rstd_b_ready, 1)
                for u in range(UPC):
                    split_hi()
                    if u == 1:
                        gate_silu(i)
                up_hi(i)

            ffn_pair(0, True)
            with repeat(act, FF // CW - 1, [(unit, 2 * UPC)]) as i:
                ffn_pair(i + 1, False)

            for _ in range(4 * (KF // UK) - LEAD):
                split_hi()

        @block.vector
        def _(dve):
            unit, own = Tally(), Tally()

            def link(instruction):
                instruction.then_inc(dve_step, 1)
                dve.wait_ge(dve_step, own.step())

            def split_lo():
                r = unit.n % RING
                dve.wait_ge(hi_ready, unit.now(1))
                nc.vector.tensor_tensor(w_lo[:, r], w_raw[:, r], w_hi[:, r].bitcast(F32), ALU.subtract).then_inc(lo_ready, 1)
                unit.step()

            def chunk_done():
                dve.wait_ge(mm_done, unit.now(-LEAD))

            def sums(p):
                return acc[p][:].rearrange("p b (n t) -> p (b n) t", t=T)

            link(nc.vector.memset(ones[:], 1.0))
            dve.wait_ge(const_in, 48)
            nc.vector.tensor_copy(ident_b[:], ident)
            nc.vector.tensor_copy(mask_b[:], mask_in[:]).then_inc(setup_done, 1)
            for t in range(TT):
                dve.wait_ge(rstd_ready, t + 1)
                nc.vector.tensor_scalar(x_row[:, t], x_row[:, t], small[:, 2 + t:3 + t], None, ALU.mult).then_inc(x_normed, 1)
            dve.wait_ge(bcast_in, 9 * 16)
            for n in range(2):
                nc.vector.tensor_tensor_reduce(out=o_sq[:, n, 0:DH], in0=bcast[:, 5 + 2 * n], in1=bcast[:, 6 + 2 * n], scale=1.0,
                                               scalar=0.0, op0=ALU.mult, op1=ALU.add,
                                               accum_out=small[:, 81 + n:82 + n]).then_inc(lam_sums, 1)
            nc.vector.tensor_copy(dt_bias_b[:], bcast[:, 0])
            nc.vector.tensor_copy(d_skip_b[:], bcast[:, 2])
            for w in range(2):
                norm_w = bcast[:, 3 + w]
                scale = DH ** -0.5 if w == 0 else 1.0
                half = DH // 2
                for t in range(TT):
                    nc.vector.scalar_tensor_tensor(out=rope[:, w, t, 0], in0=rope_in[:, t, 0], scalar=scale, in1=norm_w,
                                                   op0=ALU.mult, op1=ALU.mult)
                    for first, other in ((0, half), (half, 0)):
                        last = nc.vector.scalar_tensor_tensor(
                            out=rope[:, w, t, 1, first:first + half], in0=rope_in[:, t, 1, first:first + half], scalar=scale,
                            in1=norm_w[:, other:other + half], op0=ALU.mult, op1=ALU.mult)
            link(last)
            dve.wait_ge(lam_exps, 2)
            link(nc.vector.tensor_tensor(small[:, 85:86], small[:, 84:85], small[:, 83:84], ALU.subtract))
            link(nc.vector.tensor_scalar(small[:, 80:81], small[:, 85:86], -LAM_INIT, None, ALU.add))
            dve.wait_ge(cols_ready, 2)
            link(nc.vector.tensor_scalar(small[:, 96:97], cols[:, R_SUB:R_SUB + 1], 1.0 - LAM_INIT, None, ALU.mult))
            for b in range(KD // 2):
                dve.wait_ge(side_hi, b + 1)
                for k in (2 * b, 2 * b + 1):
                    last = nc.vector.scalar_tensor_tensor(
                        out=h_lo[:, k], in0=side[:, b % 4, (k % 2) * T:(k % 2 + 1) * T], scalar=cols[:, R_MIX + k:R_MIX + k + 1],
                        in1=h_hi[:, k].bitcast(F32), op0=ALU.mult, op1=ALU.subtract)
                last.then_inc(side_lo, 1)

            for _ in range(LEAD):
                split_lo()

            half = DH // 2

            def per_head(tile):
                return tile.rearrange("p t (h d) -> p t h d", d=DH)

            for which in range(2):
                with repeat(dve, 2, [(unit, 2 * UPC), (own, 2)]) as i:
                    for c in range(2):
                        for u in range(UPC):
                            split_lo()
                        dve.wait_ge(sq_read, i * 2 + (4 * which + c + 1))
                        nc.vector.tensor_reduce(out=small[:, 16:32], in_=sq[:].rearrange("p t (h d) -> p (t h) d", d=DH),
                                                op=ALU.add, axis=AX).then_inc(ss_ready, 1)
                        heads, main, swapped = per_head(acc[c][:]), per_head(rot_a[:]), per_head(rot_b[:])
                        shape = [P, TT, CW // DH, DH]
                        nc.vector.tensor_tensor(main, heads, rope[:, which, :, 0:1].broadcast_to(shape), ALU.mult)
                        shape = [P, TT, CW // DH, half]
                        nc.vector.tensor_tensor(swapped[..., 0:half], heads[..., half:DH],
                                                rope[:, which, :, 1:2, 0:half].broadcast_to(shape), ALU.mult)
                        nc.vector.tensor_tensor(swapped[..., half:DH], heads[..., 0:half],
                                                rope[:, which, :, 1:2, half:DH].broadcast_to(shape),
                                                ALU.mult).then_inc(acc_free[c], 1)
                        dve.wait_ge(acc_free[c], i + (2 + 2 * which))
                        link(nc.vector.tensor_tensor(rot_a[:], rot_a[:], rot_b[:], ALU.add))
                        dve.wait_ge(rstd_ready, i * 2 + (2 + 4 * which + c + 1))
                        for t in range(TT):
                            src = rot_a[:, t].rearrange("p (n s d) -> p n s d", s=2, d=DH)
                            dst = qk[:, which, bass.ds(i * 8 + c * 4, 4), t].rearrange("p n (s d) -> p n s d", d=DH)
                            rstd = small[:, 48 + 8 * t:56 + 8 * t].rearrange("p (n s) -> p n s", s=2).unsqueeze(3)
                            last = nc.vector.tensor_tensor(dst, src, rstd.broadcast_to([P, 4, 2, DH]), ALU.mult)
                        last.then_inc(qk_ready, 1)
            with repeat(dve, 2, [(unit, 2 * UPC)]) as i:
                for c in range(2):
                    for u in range(UPC):
                        split_lo()

            def conv_other_taps(c, tile, buf, first_seen, done):
                for b in range(2):
                    dve.wait_ge(conv_first, first_seen + (b + 1))
                    for back in range(1, TAPS):
                        for n in (2 * b, 2 * b + 1):
                            last = nc.vector.scalar_tensor_tensor(
                                out=buf[:, n, back:T], in0=sums(c)[:, n, 0:T - back],
                                scalar=taps[:, TAPS - 1 - back, bass.ds(tile + n, 1)], in1=buf[:, n, back:T],
                                op0=ALU.mult, op1=ALU.add)
                        if back < TAPS - 1:
                            link(last)
                last.then_inc(conv_done, 1)
                dve.wait_ge(conv_done, done)
                nc.vector.sem_inc(acc_free[c], 1)

            def row_maxes(h, b):
                dve.wait_ge(scores, h + 1 + STARTED)
                n = 32 * b
                nc.vector.tensor_reduce(out=att[:, n:n + 2], in_=side[:, 1:3, 0:P], op=ALU.max, axis=AX, negate=True)
                nc.vector.tensor_reduce(out=att[:, n + 2:n + 4], in_=side[:, 1:3, P:3 * P], op=ALU.max, axis=AX,
                                        negate=True).then_inc(max_ready, 1)

            def weights(h, b):
                dve.wait_ge(prob_ready, h + 1 + STARTED)
                dve.wait_ge(wts_T, h + STARTED)
                n = 32 * b
                link(nc.vector.reciprocal(att[:, n + 8:n + 12], att[:, n + 4:n + 8]))
                total = att[:, n + 4:n + 8].rearrange("p (q m) -> p q m", m=2)
                inverse = att[:, n + 8:n + 12].rearrange("p (q m) -> p q m", m=2)
                link(nc.vector.scalar_tensor_tensor(out=att[:, n + 12:n + 14], in0=inverse[:, :, 1], scalar=small[:, 80:81],
                                                    in1=total[:, :, 0], op0=ALU.mult, op1=ALU.mult))
                for q in range(TT):
                    cut = slice(0, P) if q == 0 else slice(P, 3 * P)
                    last = nc.vector.scalar_tensor_tensor(out=wts[:, cut], in0=prob[:, 1, cut], scalar=att[:, n + 12 + q:n + 13 + q],
                                                          in1=prob[:, 0, cut], op0=ALU.mult, op1=ALU.add)
                last.then_inc(wts_ready, 1)

            def head_output(h, b):
                dve.wait_ge(pv, h + 1 + STARTED)
                dve.wait_ge(o_T, h + STARTED)
                n = 32 * b
                for q in range(TT):
                    last = nc.vector.tensor_scalar(o_row[:, q], side[:, 3, q * P:(q + 1) * P], att[:, n + 8 + 2 * q:n + 9 + 2 * q],
                                                   None, ALU.mult)
                link(last)
                for q in range(TT):
                    last = nc.vector.tensor_tensor_reduce(out=o_sq[:, q], in0=o_row[:, q], in1=o_row[:, q], scale=1.0, scalar=0.0,
                                                          op0=ALU.mult, op1=ALU.add, accum_out=att[:, n + 14 + q:n + 15 + q])
                last.then_inc(o_sums, 1)

            def head_normed(h, b):
                dve.wait_ge(o_rstd, h + 1)
                for q in range(TT):
                    n = 32 * b + 18 + q
                    last = nc.vector.tensor_scalar(o_row[:, q], o_row[:, q], att[:, n:n + 1], None, ALU.mult)
                last.then_inc(o_ready, 1)

            def output_lo(h):
                dve.wait_ge(ya_hi_ready, h + 1)
                nc.vector.scalar_tensor_tensor(
                    out=ya_lo[:, bass.ds(h, 1)].rearrange("p o t -> p (o t)"), in0=side[:, 0, 0:T], scalar=small[:, 96:97],
                    in1=ya_hi[:, bass.ds(h, 1)].rearrange("p o t -> p (o t)").bitcast(F32),
                    op0=ALU.mult, op1=ALU.subtract).then_inc(ya_lo_ready, 1)

            def chunk_with_heads(a):
                for u in range(UPC):
                    split_lo()
                    if u == 1:
                        row_maxes(a, 0)
                    if u == 2:
                        weights(a, 0)
                    if u == 3:
                        row_maxes(a + 1, 1)
                    if u == 4:
                        weights(a + 1, 1)
                        head_output(a, 0)
                    if u == 5:
                        head_normed(a, 0)
                    if u == 6:
                        head_output(a + 1, 1)
                        output_lo(a)
                        head_normed(a + 1, 1)
                    if u == 7:
                        output_lo(a + 1)

            head_links = 2 * (2 + 1)
            conv_links = 2 * (TAPS - 2)

            with repeat(dve, 2, [(unit, 2 * UPC), (own, 2 * (head_links + conv_links))]) as i:
                for c in range(2):
                    chunk_with_heads(i * 4 + 2 * c)
                    conv_other_taps(c, i * (2 * CT) + (DI // P + c * CT), conv_a, i * 4 + 2 * c, i * 2 + (c + 1))
            with repeat(dve, 2, [(unit, 2 * UPC), (own, 2 * head_links)]) as i:
                for c in range(2):
                    chunk_with_heads(i * 4 + (8 + 2 * c))
            with repeat(dve, 2, [(unit, 2 * UPC)]) as i:
                for c in range(2):
                    for u in range(UPC):
                        split_lo()
                    chunk_done()
                    gated = merge_a[:, bass.ds(i * (2 * CT) + c * CT, CT)]
                    nc.vector.tensor_tensor(gated, sums(c), gated, ALU.mult).then_inc(acc_free[c], 1)

            def tail_gated(g):
                dve.wait_ge(y_sum, g + 1)
                dve.wait_ge(skip_ready, g + 1)
                nc.vector.tensor_tensor(y_row[:], side[:, 0:2], y_row[:], ALU.add).then_inc(y_added, 1)
                dve.wait_ge(y_added, g + 1)
                dve.wait_ge(z_ready, g + 1)
                nc.vector.tensor_tensor(y_row[:], y_row[:], z_row[:], ALU.mult).then_inc(y_gated, 1)

            def tail_normed(g):
                dve.wait_ge(y_rstd, g + 1)
                for t in range(TT):
                    last = nc.vector.tensor_scalar(y_row[:, t], y_row[:, t], small[:, 8 + t:9 + t], None, ALU.mult)
                last.then_inc(y_ready, 1)

            def tail_transposed(g):
                dve.wait_ge(y_T, g + 1)
                nc.vector.tensor_tensor(yT[:, bass.ds(g * CT, CT)], side[:, 2:4].rearrange("p b (n t) -> p (b n) t", t=T),
                                        cols[:, bass.ds(g * CT + R_SSM, CT)].unsqueeze(2).broadcast_to([P, CT, T]),
                                        ALU.mult).then_inc(yT_ready, 1)

            def steps_of_dt():
                v, mag, u, p, s, s2 = (soft[:, n] for n in range(6))
                by_tile = "p (t h) -> p t h"
                dve.wait_ge(dt_sum, 1)
                link(nc.vector.tensor_tensor(v.rearrange(by_tile, h=HS), side[:, 0, 0:TT * HS].rearrange(by_tile, h=HS),
                                             dt_bias_b[:].unsqueeze(1).broadcast_to([P, TT, HS]), ALU.add))
                nc.vector.scalar_tensor_tensor(out=mag, in0=v, scalar=-1.0, in1=v, op0=ALU.mult, op1=ALU.min).then_inc(dt_u, 1)
                dve.wait_ge(dt_exp, 1)
                link(nc.vector.tensor_scalar(p, u, 2.0, None, ALU.add))
                link(nc.vector.reciprocal(p, p))
                link(nc.vector.tensor_tensor(s, u, p, ALU.mult))
                link(nc.vector.tensor_tensor(s2, s, s, ALU.mult))
                link(nc.vector.tensor_scalar(p, s2, 1.0 / 15, None, ALU.mult))
                for odd in (13, 11, 9, 7, 5, 3):
                    link(nc.vector.scalar_tensor_tensor(out=p, in0=p, scalar=1.0 / odd, in1=s2, op0=ALU.add, op1=ALU.mult))
                link(nc.vector.scalar_tensor_tensor(out=p, in0=p, scalar=1.0, in1=s, op0=ALU.add, op1=ALU.mult))
                link(nc.vector.tensor_scalar(mag, v, 0.0, None, ALU.max))
                link(nc.vector.scalar_tensor_tensor(out=dt[:].rearrange("p t h -> p (t h)"), in0=p, scalar=2.0, in1=mag,
                                                    op0=ALU.mult, op1=ALU.add))
                nc.vector.scalar_tensor_tensor(out=dA[:], in0=dt[:], scalar=-1.0,
                                               in1=decay_rate[:].unsqueeze(1).broadcast_to([P, TT, HS]),
                                               op0=ALU.mult, op1=ALU.mult).then_inc(dA_ready, 1)

            def x_chunk(g, head):
                for u in range(UPC):
                    split_lo()
                    if head:
                        if u == 1:
                            dve.wait_ge(wdt_hi_ready, 1)
                            nc.vector.tensor_tensor(wdt_lo[:], wdt[:], wdt_hi[:].bitcast(F32), ALU.subtract).then_inc(wdt_ready, 1)
                        if u == 4:
                            steps_of_dt()
                    else:
                        if u == 2:
                            tail_gated(g - 1)
                        if u == 5:
                            tail_normed(g - 1)
                        if u == 7:
                            tail_transposed(g - 1)
                conv_other_taps(0, g * CT, conv_x, g * 2 + 8, g + 5)

            def decays(g, hf):
                dve.wait_ge(decay_exp, g * 2 + (hf + 1))
                if hf == 0:
                    dve.wait_ge(cb_ready, g + 1)
                heads = decay[:, hf * 4:hf * 4 + 4]
                nc.vector.tensor_tensor(heads, heads, cb[:].unsqueeze(1).broadcast_to([P, 4, 3 * P]), ALU.mult).then_inc(decay_ready, 1)

            def z_chunk(g):
                by_head = "p (h d) -> p h d"
                for u in range(UPC):
                    split_lo()
                    if u == 3:
                        dve.wait_ge(xs_T, g + 1)
                        for t in range(TT):
                            last = nc.vector.tensor_tensor(
                                xdt[:, t].rearrange(by_head, d=HP), side[:, 2 + t].rearrange(by_head, d=HP),
                                dt[:, t, bass.ds(g * HG, HG)].unsqueeze(2).broadcast_to([P, HG, HP]), ALU.mult)
                        last.then_inc(xdt_ready, 1)
                    if u == 4:
                        decays(g, 0)
                    if u == 7:
                        decays(g, 1)

            x_chunk(0, True)
            z_chunk(0)
            with repeat(dve, G - 1, [(unit, 2 * UPC), (own, conv_links)]) as i:
                x_chunk(i + 1, False)
                z_chunk(i + 1)

            for c in range(4):
                for u in range(UPC):
                    split_lo()
                    if c == 0 and u == 2:
                        tail_gated(G - 1)
                    if c == 0 and u == 5:
                        tail_normed(G - 1)
                    if c == 0 and u == 7:
                        tail_transposed(G - 1)
                    if c and u in (1, 3, 5) and 3 * (c - 1) + u // 2 < KI // 4:
                        n = 3 * (c - 1) + u // 2
                        dve.wait_ge(y_hi_ready, n + 1)
                        cut = slice(4 * n, 4 * n + 4)
                        nc.vector.tensor_tensor(y_lo[:, cut], yT[:, cut], y_hi[:, cut].bitcast(F32), ALU.subtract).then_inc(y_lo_ready, 1)

            with repeat(dve, 2, [(unit, 4 * UPC), (own, 2)]) as i:
                for c in range(2):
                    for u in range(2 * UPC):
                        split_lo()
                    chunk_done()
                    cut = bass.ds(i * (2 * CT) + c * CT, CT)
                    link(nc.vector.tensor_tensor(m_row[:], sums(c), gate_s[:, cut], ALU.mult))
                    nc.vector.sem_inc(acc_free[c], 1)
                    nc.vector.tensor_tensor(m_row[:], m_row[:], merge_a[:, cut], ALU.add).then_inc(m_ready, 1)
                    dve.wait_ge(m_hi_ready, i * 2 + (c + 1))
                    nc.vector.tensor_tensor(m_lo[:, cut], m_row[:], m_hi[:, cut].bitcast(F32), ALU.subtract).then_inc(m_lo_ready, 1)

            def residual_lo(c):
                dve.wait_ge(x2_hi_ready, c + 1)
                for n in range(CT):
                    k = c * CT + n
                    last = nc.vector.scalar_tensor_tensor(
                        out=x2T_lo[:, k], in0=side[:, 2:4].rearrange("p b (n t) -> p (b n) t", t=T)[:, n],
                        scalar=cols[:, R_FFN + k:R_FFN + k + 1], in1=x2T_hi[:, k].bitcast(F32), op0=ALU.mult, op1=ALU.subtract)
                last.then_inc(x2_lo_ready, 1)

            dve.wait_ge(x2_in, 16)
            for c in range(D // CW):
                for u in range(UPC):
                    split_lo()
                    if c and u == 4:
                        residual_lo(c - 1)
                chunk_done()
                cut = slice(c * CW, (c + 1) * CW)
                nc.vector.tensor_tensor(x2[:, :, cut], acc[c % 2][:], x2[:, :, cut], ALU.add).then_inc(x2_ready, 1)
                dve.wait_ge(x2_ready, c + 1)
                nc.vector.sem_inc(acc_free[c % 2], 1)

            def ffn_pair(i, head):
                for u in range(UPC):
                    split_lo()
                    if head and u == 3:
                        residual_lo(D // CW - 1)
                    if head and u == 5:
                        dve.wait_ge(x2_rstd, 1)
                        for t in range(TT):
                            last = nc.vector.tensor_scalar(diag[:, t], ident, small[:, 88 + t:89 + t], None, ALU.mult)
                        last.then_inc(diag_ready, 1)
                if head:
                    dve.wait_ge(rstd_b_ready, 1)
                rstd = rstd_b[:].unsqueeze(1).broadcast_to([P, CT, T])
                chunk_done()
                nc.vector.tensor_tensor(gate_f[:], sums(0), rstd, ALU.mult).then_inc(gate_f_scaled, 1)
                dve.wait_ge(gate_f_scaled, i + 1)
                nc.vector.sem_inc(acc_free[0], 1)
                for u in range(UPC):
                    split_lo()
                chunk_done()
                link(nc.vector.tensor_tensor(up_f[:], sums(1), rstd, ALU.mult))
                nc.vector.sem_inc(acc_free[1], 1)
                dve.wait_ge(gate_f_ready, i + 1)
                nc.vector.tensor_tensor(up_f[:], up_f[:], gate_f[:], ALU.mult).then_inc(a_ready, 1)
                cut = bass.ds(i * CT, CT)
                dve.wait_ge(a_hi_ready, i + 1)
                nc.vector.tensor_tensor(a_lo[:, cut], up_f[:], a_hi[:, cut].bitcast(F32), ALU.subtract).then_inc(a_lo_ready, 1)

            ffn_pair(0, True)
            with repeat(dve, FF // CW - 1, [(unit, 2 * UPC), (own, 1)]) as i:
                ffn_pair(i + 1, False)

            for c in range(D // CW):
                final = c == D // CW - 1
                for u in range(KF // UK - (LEAD if final else 0)):
                    split_lo()
                dve.wait_ge(mm_done, unit.now(0 if final else -LEAD))
                if c >= 2:
                    dve.wait_ge(out_done[c % 2], 16)
                cut = slice(c * CW, (c + 1) * CW)
                nc.vector.tensor_tensor(out_row[:, c % 2], acc[c % 2][:], x2[:, :, cut], ALU.add).then_inc(out_ready, 1)
                dve.wait_ge(out_ready, c + 1)
                nc.vector.sem_inc(acc_free[c % 2], 1)

        @block.gpsimd
        def _(pool):
            own = Tally()

            def rsqrt(out, mean_of, sums_at, tmp, eps):
                n = sums_at.shape[1]
                nc.gpsimd.tensor_tensor(tmp, sums_at, constant[1 / mean_of][:, 0:n], ALU.mult).then_inc(pool_step, 1)
                pool.wait_ge(pool_step, own.step())
                nc.gpsimd.tensor_tensor(tmp, tmp, constant[eps][:, 0:n], ALU.add).then_inc(pool_step, 1)
                pool.wait_ge(pool_step, own.step())
                return nc.gpsimd.tensor_tensor(out, tmp, small[:, 64:64 + sums_at.shape[1]], ALU.pow)

            constant = {}
            for n, value in enumerate((1 / D, 1 / DH, 1 / (2 * DH), 1 / CW, NORM_EPS, SUBLN_EPS)):
                constant[value] = pool_constants[:, n]
                nc.gpsimd.memset(constant[value], value)
            nc.gpsimd.memset(small[:, 64:80], -0.5).then_inc(pool_step, 1)
            pool.wait_ge(pool_step, own.step())
            for t in range(TT):
                pool.wait_ge(ss_ready, t + 1)
                rsqrt(small[:, 2 + t:3 + t], D, small[:, t:t + 1], small[:, 92 + t:93 + t], NORM_EPS).then_inc(rstd_ready, 1)
            with repeat(pool, 2 * D // CW, [(own, 2)]) as i:
                pool.wait_ge(ss_ready, i + (TT + 1))
                rsqrt(small[:, 48:64], DH, small[:, 16:32], small[:, 32:48], NORM_EPS).then_inc(rstd_ready, 1)
            with repeat(pool, NA // 2, [(own, 4)]) as i:
                for b in range(2):
                    pool.wait_ge(o_sums, i * 2 + (b + 1) + STARTED)
                    n = 32 * b
                    rsqrt(att[:, n + 18:n + 20], 2 * DH, att[:, n + 14:n + 16], att[:, n + 16:n + 18], SUBLN_EPS).then_inc(o_rstd, 1)

            def tail(g):
                pool.wait_ge(y_squared, g + 1)
                rsqrt(small[:, 8:10], CW, small[:, 4:6], small[:, 6:8], SUBLN_EPS).then_inc(y_rstd, 1)

            def loads(g):
                for hf in range(2):
                    heads = acs_dram[bass.ds(g * HG + hf * 4, 4), :]
                    pool.dma_start(acs_b[:, hf], heads.partition_broadcast(P)).then_inc(acs_in[hf], 16)

            def group(g):
                mask = mask_sl.unsqueeze(1).broadcast_to([P, 4, P])
                for hf in range(2):
                    pool.wait_ge(acs_in[hf], g * 16 + 16)
                    nc.gpsimd.tensor_tensor(acs_m[:, hf], acs_b[:, hf, :, P:T], mask, ALU.add).then_inc(acs_masked, 1)
                    nc.gpsimd.tensor_tensor(acs_b[:, hf, :, 0:P], acs_b[:, hf, :, 0:P], mask, ALU.add).then_inc(acs_masked, 1)
                by_head = "p (h d) -> p h d"
                pool.wait_ge(xrow_ready, g + 1)
                for t in range(TT):
                    x_heads = y_row[:, t].rearrange(by_head, d=HP)
                    last = nc.gpsimd.tensor_tensor(
                        x_heads, x_heads, d_skip_b[:, bass.ds(g * HG, HG)].unsqueeze(2).broadcast_to([P, HG, HP]), ALU.mult)
                last.then_inc(skip_ready, 1)

            pool.wait_ge(acs_ready, 2)
            pool.dma_start(acs_dram[:], acsT[:]).then_inc(acs_out, 16)
            pool.wait_ge(acs_out, 16)
            loads(0)
            group(0)
            with repeat(pool, G - 1, [(own, 2)]) as i:
                pool.wait_ge(decay_exp, i * 2 + 2)
                loads(i + 1)
                tail(i)
                group(i + 1)
            tail(G - 1)
            pool.wait_ge(x2_ss, 1)
            rsqrt(small[:, 88:90], D, small[:, 86:88], small[:, 90:92], NORM_EPS).then_inc(x2_rstd, 1)

        @block.tensor
        def _(pe):
            unit, pair = Tally(), Tally()

            def rows_unit(p, k0, stat_hi, stat_lo, first, last):
                r = unit.n % RING
                pe.wait_ge(lo_ready, unit.step())
                for kk in range(UK):
                    for t in range(TT):
                        cut = slice(t * P, (t + 1) * P)
                        for n, (a, w) in enumerate(((stat_hi, w_hi), (stat_hi, w_lo), (stat_lo, w_hi))):
                            done = nc.tensor.matmul(acc[p][:, t], a[:, k0 + kk, cut], w[:, r, kk], start=first and kk == n == 0,
                                                    stop=last and kk == UK - 1 and n == 2)
                done.then_inc(mm_done, 1)

            def cols_unit(p, k0, mov_hi, mov_lo, first, last):
                r = unit.n % RING
                pe.wait_ge(lo_ready, unit.step())
                for kk in range(UK):
                    for c in range(CT):
                        out_at = acc[p][:, c // 2, (c % 2) * T:(c % 2 + 1) * T]
                        cut = slice(c * P, (c + 1) * P)
                        for n, (w, a) in enumerate(((w_hi, mov_hi), (w_hi, mov_lo), (w_lo, mov_hi))):
                            done = nc.tensor.matmul(out_at, w[:, r, kk, cut], a[:, k0 + kk], start=first and kk == n == 0 and c % 2 == 0,
                                                    stop=last and kk == UK - 1 and n == 2, skip_group_check=True)
                done.then_inc(mm_done, 1)

            def chunk(kind, p, hi, lo, units=UPC, between=None):
                pe.wait_ge(acc_free[p], pair.now(1))
                for u in range(units):
                    kind(p, u * UK, hi, lo, u == 0, u == units - 1)
                    if between is not None:
                        between(u)
                if p:
                    pair.step()

            def transpose(out_at, in_):
                return nc.tensor.transpose(out_at, in_, ident)

            pe.wait_ge(const_in, 48)
            pe.wait_ge(rows_in, 7 * 16)
            nc.tensor.transpose(side[:, 0, 0:R_CONV], rows[0:R_CONV, 0], ident[0:R_CONV, 0:R_CONV])
            nc.tensor.transpose(side[:, 0, R_CONV:2 * R_CONV], rows[0:R_CONV, 1], ident[0:R_CONV, 0:R_CONV])
            nc.tensor.transpose(side[:, 0, 2 * R_CONV:2 * R_CONV + R_ALL], rows[0:R_ALL, 2],
                                ident[0:R_ALL, 0:R_ALL]).then_inc(rows_T, 1)
            pe.wait_ge(x_normed, TT)
            pe.wait_ge(setup_done, 1)
            pe.wait_ge(cols_ready, 2)
            for b in range(KD // 2):
                if b >= 4:
                    pe.wait_ge(side_lo, b - 3)
                for k in (2 * b, 2 * b + 1):
                    for t in range(TT):
                        at_col = (k % 2) * T + t * P
                        last = transpose(side[:, b % 4, at_col:at_col + P], x_row[:, t, k * P:(k + 1) * P])
                last.then_inc(side_T, 1)
            pe.wait_ge(side_lo, KD // 2)

            with repeat(pe, 6, [(unit, 2 * UPC), (pair, 1)]) as i:
                for c in range(2):
                    chunk(rows_unit, c, h_hi, h_lo)

            def head_rows(h, b):
                for w in range(2):
                    for t in range(TT):
                        n = w * TT + t
                        last = transpose(side[:, 0, n * P:(n + 1) * P], qk_row[:, b, w, t])
                last.then_inc(qk_T, 1)

            def head_scores(h):
                pe.wait_ge(qkT_ready, h + 1)
                pe.wait_ge(prob_ready, h + STARTED)
                for m in range(2):
                    half = slice(m * DH, (m + 1) * DH)
                    for q in range(TT):
                        first, width = q * P, (q + 1) * P
                        nc.tensor.matmul(side[:, 1 + m, first:first + width], qkT[half, 0, q * P:(q + 1) * P],
                                         qkT[half, 1, 0:width], start=True, stop=False)
                        last = nc.tensor.matmul(side[:, 1 + m, first + width - P:first + width], ident_b[:], mask_b[:],
                                                start=False, stop=True)
                last.then_inc(scores, 1)

            def head_weights(h):
                pe.wait_ge(wts_ready, h + 1 + STARTED)
                for n in range(3):
                    last = transpose(side[:, 0, n * P:(n + 1) * P], wts[:, n * P:(n + 1) * P])
                last.then_inc(wts_T, 1)

            def head_values(h):
                pe.wait_ge(wtsT_ready, h + 1)
                pe.wait_ge(o_sums, h + STARTED)
                v0, v1 = (v_all[:, t, bass.ds(h * P, P)] for t in range(TT))
                nc.tensor.matmul(side[:, 3, 0:P], wtsT[:, 0:P], v0, start=True, stop=True)
                nc.tensor.matmul(side[:, 3, P:2 * P], wtsT[:, P:2 * P], v0, start=True, stop=False)
                nc.tensor.matmul(side[:, 3, P:2 * P], wtsT[:, 2 * P:3 * P], v1, start=False, stop=True).then_inc(pv, 1)

            def head_out(h):
                pe.wait_ge(o_ready, h + 1)
                for t in range(TT):
                    last = transpose(side[:, 0, t * P:(t + 1) * P], o_row[:, t])
                last.then_inc(o_T, 1)

            def heads_between(a):
                def between(u):
                    if u == 0:
                        pe.wait_ge(row_in[0], a * 8 + 16)
                        pe.wait_ge(ya_lo_ready, a + STARTED)
                        head_rows(a, 0)
                    if u == 1:
                        head_scores(a)
                    if u == 2:
                        pe.wait_ge(row_in[1], a * 8 + 16)
                        head_rows(a + 1, 1)
                    if u == 3:
                        pe.wait_ge(qkT_ready, a + 2)
                        head_weights(a)
                        head_scores(a + 1)
                    if u == 4:
                        head_values(a)
                    if u == 5:
                        head_weights(a + 1)
                    if u == 6:
                        head_values(a + 1)
                        head_out(a)
                    if u == 7:
                        pe.wait_ge(ya_lo_ready, a + 1 + STARTED)
                        head_out(a + 1)
                return between

            for n in range(2):
                with repeat(pe, 2, [(unit, 2 * UPC), (pair, 1)]) as i:
                    for c in range(2):
                        chunk(cols_unit, c, h_hi, h_lo, between=heads_between(i * 4 + (8 * n + 2 * c)))
            def last_heads(u):
                if u == UPC - 2:
                    pe.wait_ge(ya_lo_ready, NA + STARTED)

            pe.wait_ge(ya_lo_ready, NA - UK + STARTED)
            with repeat(pe, 2, [(unit, 2 * UPC), (pair, 1)]) as i:
                for c in range(2):
                    chunk(cols_unit, c, ya_hi, ya_lo, between=last_heads)

            def dt_products():
                pe.wait_ge(wdt_ready, 1)
                for t in range(TT):
                    cut = slice(t * P, (t + 1) * P)
                    for k in range(KD):
                        for n, (a, w) in enumerate(((h_hi, wdt_hi), (h_hi, wdt_lo), (h_lo, wdt_hi))):
                            last = nc.tensor.matmul(side[:, 0, t * HS:(t + 1) * HS], a[:, k, cut], w[:, k],
                                                    start=k == n == 0, stop=k == KD - 1 and n == 2)
                last.then_inc(dt_sum, 1)

            def cumulative():
                pe.wait_ge(dA_ready, 1)
                nc.tensor.matmul(side[:, 1, 0:HS], tri, dA[:, 0], start=True, stop=True)
                nc.tensor.matmul(side[:, 1, HS:2 * HS], ones[:], dA[:, 0], start=True, stop=False)
                nc.tensor.matmul(side[:, 1, HS:2 * HS], tri, dA[:, 1], start=False, stop=True)
                nc.tensor.matmul(side[0:HS, 2, 0:P], dA[:, 0], tri, start=True, stop=True)
                nc.tensor.matmul(side[0:HS, 2, P:T], dA[:, 0], ones[:], start=True, stop=False)
                nc.tensor.matmul(side[0:HS, 2, P:T], dA[:, 1], tri, start=False, stop=True).then_inc(acs_sum, 1)

            def y_products(g, hf):
                if hf == 0:
                    pe.wait_ge(decay_ready, g * 2 + 2)
                    pe.wait_ge(xdt_ready, g + 1)
                    pe.wait_ge(cb_ready, g + 1)
                for h in range(hf * 4, hf * 4 + 4):
                    cut = slice(h * HP, (h + 1) * HP)
                    nc.tensor.matmul(side[:, 0, cut], decay[:, h, 0:P], xdt[:, 0, cut], start=True, stop=True)
                    nc.tensor.matmul(side[:, 1, cut], decay[:, h, P:T], xdt[:, 0, cut], start=True, stop=False)
                    last = nc.tensor.matmul(side[:, 1, cut], decay[:, h, T:T + P], xdt[:, 1, cut], start=False, stop=True)
                if hf:
                    last.then_inc(y_sum, 1)

            def to_columns(tile, first):
                for n in range(CT):
                    for t in range(TT):
                        at_col = (n % 2) * T + t * P
                        last = transpose(side[:, 2 + n // 2, at_col:at_col + P], tile[:, t, first + n * P:first + (n + 1) * P])
                return last

            def tail_between(g):
                def between(u):
                    if u in (0, 1):
                        y_products(g, u)
                    if u == 6:
                        pe.wait_ge(y_ready, g + 1)
                        pe.wait_ge(xrow_ready, g + 1)
                        to_columns(y_row, 0).then_inc(y_T, 1)
                return between

            def first_between(u):
                if u == 2:
                    dt_products()
                if u == 6:
                    cumulative()

            def z_between(g, first=False):
                def between(u):
                    if u == 0:
                        pe.wait_ge(bT_ready, g + 1)
                        if first:
                            pe.wait_ge(acs_ready, 2)
                        else:
                            pe.wait_ge(y_added, g)
                        c_rows = bc[:, bass.ds(g + G, 1)].rearrange("p o t -> p (o t)")
                        c_late = bc[:, bass.ds(g + G, 1), P:T].rearrange("p o t -> p (o t)")
                        nc.tensor.matmul(side[:, 0, 0:T], bT[:, 0:P], c_rows, start=True, stop=True)
                        nc.tensor.matmul(side[:, 0, T:T + P], bT[:, P:T], c_late, start=True, stop=True).then_inc(cb_sum, 1)
                    if u == 2:
                        pe.wait_ge(xs_ready, g + 1)
                        if not first:
                            pe.wait_ge(yT_ready, g)
                        for n in range(CT):
                            for t in range(TT):
                                last = transpose(side[:, 2 + t, n * P:(n + 1) * P], conv_x[:, n, t * P:(t + 1) * P])
                        last.then_inc(xs_T, 1)
                return between

            chunk(cols_unit, 0, h_hi, h_lo, between=first_between)
            chunk(rows_unit, 1, h_hi, h_lo, between=z_between(0, True))
            with repeat(pe, G - 1, [(unit, 2 * UPC), (pair, 1)]) as i:
                chunk(cols_unit, 0, h_hi, h_lo, between=tail_between(i))
                chunk(rows_unit, 1, h_hi, h_lo, between=z_between(i + 1))
            for c in range(D // CW):
                chunk(cols_unit, c % 2, h_hi, h_lo, between=tail_between(G - 1) if c == 0 else None)
            pe.wait_ge(y_lo_ready, KI // 4)
            with repeat(pe, 2, [(unit, 4 * UPC), (pair, 1)]) as i:
                for c in range(2):
                    chunk(cols_unit, c, y_hi, y_lo, 2 * UPC)

            def residual_columns(c):
                pe.wait_ge(x2_ready, c + 1)
                if c:
                    pe.wait_ge(x2_lo_ready, c)
                else:
                    pe.wait_ge(yT_ready, G)
                to_columns(x2, c * CW).then_inc(x2_T, 1)

            def out_between(c):
                def between(u):
                    if c == 0 and u == UPC - 3:
                        pe.wait_ge(m_lo_ready, 4)
                    if c and u == 3:
                        residual_columns(c - 1)
                return between

            pe.wait_ge(m_lo_ready, 3)
            for c in range(D // CW):
                chunk(rows_unit, c % 2, m_hi, m_lo, between=out_between(c))

            def first_ffn(u):
                if u == 1:
                    residual_columns(3)
                if u == UPC - 3:
                    pe.wait_ge(x2_lo_ready, 4)
                if u == 5:
                    pe.wait_ge(diag_ready, 1)
                    for t in range(TT):
                        last = nc.tensor.matmul(side[:, 0, t * P:(t + 1) * P], ones[:], diag[:, t], start=True, stop=True)
                    last.then_inc(rstd_T, 1)

            pe.wait_ge(x2_lo_ready, 3)
            chunk(cols_unit, 0, x2T_hi, x2T_lo, between=first_ffn)
            chunk(cols_unit, 1, x2T_hi, x2T_lo)
            with repeat(pe, FF // CW - 1, [(unit, 2 * UPC), (pair, 1)]) as i:
                for c in range(2):
                    chunk(cols_unit, c, x2T_hi, x2T_lo)

            def last_ffn(u):
                if u == KF // UK - 3:
                    pe.wait_ge(a_lo_ready, FF // CW)

            pe.wait_ge(a_lo_ready, FF // CW - 1)
            with repeat(pe, 2, [(unit, KF), (pair, 1)]) as i:
                for c in range(2):
                    chunk(rows_unit, c, a_hi, a_lo, KF // UK, between=last_ffn)


def kernel(**inputs):
    import concourse.bacc as bacc
    from concourse.bass_utils import run_bass_kernel_spmd

    nc = bacc.Bacc("TRN2", target_bir_lowering=False, num_devices=1)
    names = ("x", "mix_norm_w", "w_in", "conv_w", "conv_b", "dt_bias", "a_log", "d_skip", "ssm_norm_w", "w_ssm_proj",
             "q_norm_w", "k_norm_w", "lambda_q1", "lambda_k1", "lambda_q2", "lambda_k2", "subln_w", "w_attn_proj",
             "w_out", "ffn_norm_w", "w_ffn_gate", "w_ffn_up", "w_ffn_down")
    arrays = {f"in_{n}": np.ascontiguousarray(inputs[n]) for n in names}
    arrays["in_consts"] = constants()
    aps = [nc.dram_tensor(n, a.shape, F32, kind="ExternalInput").ap() for n, a in arrays.items()]
    out = nc.dram_tensor("out", (1, T, D), F32, kind="ExternalOutput").ap()
    layer(nc, *aps, out)
    result = run_bass_kernel_spmd(nc, [arrays], core_ids=[0])
    return result.results[0]["out"]
```

```python
from contextlib import ExitStack, contextmanager

import concourse.bass as bass
import numpy as np
from concourse import mybir

F32 = mybir.dt.float32
F32R = mybir.dt.float32r
BF16 = mybir.dt.bfloat16
ALU = mybir.AluOpType
ACT = mybir.ActivationFunctionType
AX = mybir.AxisListType.X

P = 128
T = 256
TT = T // P
D = 2048
KD = D // P
DI = 2 * D
KI = DI // P
HS = 64
HP = 64
G = 8
HG = HS // G
NS = 128
TAPS = 4
XBC = DI + 2 * G * NS
NA = 16
DH = 64
STARTED = 2
FF = 5632
KF = FF // P
CW = 512
CT = CW // P
UK = 2
RING = 4
LEAD = 4
UPC = KD // UK

WARM_START, WARM_TILE, WARM_UNIT = 24, 4, 8

COL_Z = 0
COL_X = DI
COL_BC = COL_X + DI
COL_DT = COL_X + XBC
COL_Q = COL_DT + HS
COL_K = COL_Q + D
COL_V = COL_K + D
COL_GS = COL_V + D
COL_GA = COL_GS + D

NORM_EPS = 1e-6
SUBLN_EPS = 1e-5
LAM_INIT = 0.8 - 0.6 * float(np.exp(-0.3 * 0))
MASKED = -1e30

MAX, SUM, INVERSE, RATIO, SQUARES, SCRATCH, RSTD, ATT_COLUMNS = 0, 4, 8, 12, 14, 16, 18, 32

C_ID, C_TRI, C_MASK_SL, C_MASK_QK, C_ROPE = 0, P, 2 * P, 3 * P, 4 * P
C_ALL = C_ROPE + TT * 2 * DH

R_CONV = 2 * (XBC // P)
R_BIAS, R_MIX = 0, XBC // P
R_FFN, R_SSM = R_MIX + KD, R_MIX + 2 * KD
R_SUB = R_SSM + KI
R_ALL = R_SUB + 1


def constants():
    c = np.zeros((P, C_ALL), np.float32)
    c[:, C_ID:C_ID + P] = np.eye(P, dtype=np.float32)
    row, col = np.arange(P)[:, None], np.arange(P)[None, :]
    c[:, C_TRI:C_TRI + P] = (row <= col)
    c[:, C_MASK_SL:C_MASK_SL + P] = np.where(row <= col, 0.0, MASKED)
    c[:, C_MASK_QK:C_MASK_QK + P] = np.where(col <= row, 0.0, MASKED)
    half = DH // 2
    inv = np.float32(10000.0) ** (-np.arange(half, dtype=np.float32) / np.float32(half))
    angle = np.arange(T, dtype=np.float32)[:, None] * inv.astype(np.float32)[None, :]
    cos, sin = np.cos(angle).astype(np.float32), np.sin(angle).astype(np.float32)
    for t in range(TT):
        r = slice(t * P, (t + 1) * P)
        at = C_ROPE + t * 2 * DH
        c[:, at:at + 2 * DH] = np.concatenate([cos[r], cos[r], -sin[r], sin[r]], axis=1)
    return c


class Tally:

    def __init__(self):
        self.base, self.n = 0, 0

    def step(self, k=1):
        self.n += k
        return self.base + self.n

    def now(self, k=0):
        return self.base + self.n + k


@contextmanager
def repeat(engine, times, counts):
    before = [t.n for t, _ in counts]
    with engine.Fori(0, times) as i:
        for (t, per), n in zip(counts, before):
            t.base, t.n = i * per + n, 0
        yield i
        for t, per in counts:
            assert t.n == per, (t.n, per)
    for (t, per), n in zip(counts, before):
        t.base, t.n = 0, n + times * per


def layer(nc, x, mix_norm_w, w_in, conv_w, conv_b, dt_bias, a_log, d_skip, ssm_norm_w, w_ssm_proj,
          q_norm_w, k_norm_w, lambda_q1, lambda_k1, lambda_q2, lambda_k2, subln_w, w_attn_proj,
          w_out, ffn_norm_w, w_ffn_gate, w_ffn_up, w_ffn_down, consts, out):
    ctx = ExitStack()
    with ctx:
        base = -(-nc.sbuf_base // 64) * 64

        def at(name, kb, shape, dtype=F32):
            return nc.alloc_sbuf_tensor_at(name, shape, dtype, offset=base + int(kb * 1024))

        def sem(name):
            return ctx.enter_context(nc.semaphore(name))

        w_raw = at("w_raw", 0, [P, RING, UK, CW])
        w_hi = at("w_hi", 16, [P, RING, UK, CW], F32R)
        w_lo = at("w_lo", 32, [P, RING, UK, CW], F32R)
        h_hi = at("h_hi", 48, [P, KD, T], F32R)
        h_lo = at("h_lo", 64, [P, KD, T], F32R)
        x2T_hi = at("x2T_hi", 48, [P, KD, T], F32R)
        x2T_lo = at("x2T_lo", 64, [P, KD, T], F32R)
        cst = at("cst", 80, [P, 3 * P])
        ident, tri, mask_sl = (cst[:, a:a + P] for a in (C_ID, C_TRI, C_MASK_SL))
        ones = at("ones", 81.5, [P, P])
        ident_b = at("ident_b", 82, [P, P], BF16)
        mask_b = at("mask_b", 82.25, [P, P], BF16)
        taps = at("taps", 82.5, [P, TAPS, XBC // P])
        cols = at("cols", 83.25, [P, P])
        dt_bias_b = at("dt_bias_b", 83.75, [P, HS])
        decay_rate = at("decay_rate", 84, [P, HS])
        d_skip_b = at("d_skip_b", 84.25, [P, HS])
        dt = at("dt", 84.5, [P, TT, HS])
        dA = at("dA", 85, [P, TT, HS])
        neg_acs = at("neg_acs", 85.5, [P, TT, HS])
        small = at("small", 86, [P, 128])
        (x_ss, x_scratch, x_rstd, y_ss, y_scratch, y_scale, x2_sums, x2_scratch, x2_scale, lam_dots, lam_parts) = (
            small[:, TT * n:TT * (n + 1)] for n in range(11))
        minus_lam, subln_scale = small[:, 22:23], small[:, 23:24]
        qk_ss, qk_scratch, qk_rstd, power = (small[:, 32 + 16 * n:48 + 16 * n] for n in range(4))
        pool_constants = at("pool_constants", 86.5, [P, 6, 16])
        qk = at("qk", 87, [P, 2, NA, TT, P])
        ya_hi = at("ya_hi", 87, [P, KD, T], F32R)
        ya_lo = at("ya_lo", 103, [P, KD, T], F32R)
        v_all = at("v_all", 119, [P, TT, D])
        bc_raw = at("bc_raw", 135, [P, 2 * G, T])
        bc = at("bc", 119, [P, 2 * G, T])
        merge_a = at("merge_a", 151, [P, KD, T])
        sq = at("sq", 167, [P, TT, CW])
        rot_a = at("rot_a", 171, [P, TT, CW])
        rot_b = at("rot_b", 175, [P, TT, CW])
        rope = at("rope", 179, [P, 2, TT, 2, DH])
        qk_row = at("qk_row", 181, [P, 2, 2, TT, P])
        qkT = at("qkT", 185, [P, 2, T])
        prob = at("prob", 187, [P, 2, 3 * P])
        wts = at("wts", 190, [P, 3 * P])
        wtsT = at("wtsT", 191.5, [P, 3 * P])
        o_row = at("o_row", 193, [P, 2, TT, P])
        o_sq = at("o_sq", 198, [P, TT, P])
        att = at("att", 199, [P, 2 * ATT_COLUMNS])
        rows = at("rows", 200, [P, 3, P])
        bcast = at("bcast", 202, [P, 9, HS])
        x_row = at("x_row", 119, [P, TT, D])
        rope_in = at("rope_in", 205, [P, TT, 2, DH])
        mask_in = at("mask_in", 206, [P, P])
        yT = at("yT", 87, [P, KI, T])
        y_lo = at("y_lo", 87, [P, KI, T], F32R)
        y_hi = at("y_hi", 119, [P, KI, T], F32R)
        wdt = at("wdt", 167, [P, KD, HS])
        wdt_hi = at("wdt_hi", 171, [P, KD, HS], F32R)
        wdt_lo = at("wdt_lo", 175, [P, KD, HS], F32R)
        decay = at("decay", 167, [P, HG, TT, P])
        edge = at("edge", 135, [P, TT, HS])
        xdt_end = at("xdt_end", 136, [P, CW])
        after = at("after", 201, [P, P])
        acs_b = at("acs_b", 179, [P, 2, HG // 2, T])
        conv_x = at("conv_x", 191, [P, CT, T])
        y_row = at("y_row", 195, [P, TT, CW])
        xdt = at("xdt", 199, [P, TT, CW])
        z_row = at("z_row", 203, [P, TT, CW])
        bT = at("bT", 147, [P, T])
        cb = at("cb", 148, [P, 3 * P])
        acsT = at("acsT", 185, [HS, T])
        dtT = at("dtT", 200, [HS, T])
        soft = at("soft", 167, [P, 6, TT * HS])
        gate_s = at("gate_s", 167, [P, KD, T])
        m_hi = at("m_hi", 151, [P, KD, T], F32R)
        m_lo = at("m_lo", 167, [P, KD, T], F32R)
        m_row = at("m_row", 199, [P, CT, T])
        x2 = at("x2", 183, [P, TT, D])
        a_hi = at("a_hi", 87, [P, KF, T], F32R)
        a_lo = at("a_lo", 131, [P, KF, T], F32R)
        gate_f = at("gate_f", 175, [P, CT, T])
        up_f = at("up_f", 179, [P, CT, T])
        rstd_b = at("rstd_b", 203, [P, T])
        x2_sq = at("x2_sq", 87, [P, TT, D])
        diag = at("diag", 204, [P, TT, P])
        out_row = at("out_row", 175, [P, 2, TT, CW])

        acs_dram = nc.dram_tensor("acs_scratch", (HS, T), F32, kind="Internal").ap()

        acc = [ctx.enter_context(nc.psum_tensor(f"acc{p}", [P, 2, CW], F32)) for p in range(2)]
        side = ctx.enter_context(nc.psum_tensor("side", [P, 4, CW], F32))

        raw_in = [sem(f"raw_in{r}") for r in range(RING)]
        hi_ready = sem("hi_ready")
        lo_ready = sem("lo_ready")
        mm_done = sem("mm_done")
        acc_free = [sem(f"acc_free{p}") for p in range(2)]
        const_in, rows_in, bcast_in, tables_in = sem("const_in"), sem("rows_in"), sem("bcast_in"), sem("tables_in")
        x_in = [sem(f"x_in{t}") for t in range(TT)]
        dve_step, pool_step = sem("dve_step"), sem("pool_step")
        ss_ready, rstd_ready = sem("ss_ready"), sem("rstd_ready")
        x_normed, side_T, side_hi, side_lo = sem("x_normed"), sem("side_T"), sem("side_hi"), sem("side_lo")
        ones_ready = sem("ones_ready")
        rows_T, cols_ready, setup_done = sem("rows_T"), sem("cols_ready"), sem("setup_done")
        lam_sums, lam_exps = sem("lam_sums"), sem("lam_exps")
        conv_first, conv_done = sem("conv_first"), sem("conv_done")
        sq_read = sem("sq_read")
        bc_first, bc_conv, bc_ready = sem("bc_first"), sem("bc_conv"), sem("bc_ready")
        row_in = [sem(f"row_in{a}") for a in range(2)]
        qk_T, qkT_ready, scores, max_ready = sem("qk_T"), sem("qkT_ready"), sem("scores"), sem("max_ready")
        prob_ready, wts_ready, wts_T, wtsT_ready = sem("prob_ready"), sem("wts_ready"), sem("wts_T"), sem("wtsT_ready")
        pv, o_sums, o_rstd, o_ready, o_T = sem("pv"), sem("o_sums"), sem("o_rstd"), sem("o_ready"), sem("o_T")
        ya_hi_ready, ya_lo_ready, qk_ready = sem("ya_hi_ready"), sem("ya_lo_ready"), sem("qk_ready")
        wdt_in, wdt_hi_ready, wdt_ready, dt_sum, dt_u, dt_exp = (sem(n) for n in (
            "wdt_in", "wdt_hi_ready", "wdt_ready", "dt_sum", "dt_u", "dt_exp"))
        dtT_sum, dtT_ready = sem("dtT_sum"), sem("dtT_ready")
        dA_ready, acs_sum, acs_ready, acs_out = sem("dA_ready"), sem("acs_sum"), sem("acs_ready"), sem("acs_out")
        acs_in = [sem(f"acs_in{h}") for h in range(2)]
        acs_masked, decay_exp, decay_ready = sem("acs_masked"), sem("decay_exp"), sem("decay_ready")
        after_ready, edge_ready, xdt_end_ready, late_ready = (sem(n) for n in ("after_ready", "edge_ready", "xdt_end_ready", "late_ready"))
        bT_ready, cb_sum, cb_ready = sem("bT_ready"), sem("cb_sum"), sem("cb_ready")
        xs_ready, xs_T, xdt_ready, xrow_ready, skip_ready = (sem(n) for n in (
            "xs_ready", "xs_T", "xdt_ready", "xrow_ready", "skip_ready"))
        z_ready, y_sum, y_gated, y_squared, y_rstd, y_ready, y_T, yT_ready = (sem(n) for n in (
            "z_ready", "y_sum", "y_gated", "y_squared", "y_rstd", "y_ready", "y_T", "yT_ready"))
        y_hi_ready, y_lo_ready, y_added = sem("y_hi_ready"), sem("y_lo_ready"), sem("y_added")
        m_ready, m_hi_ready, m_lo_ready = sem("m_ready"), sem("m_hi_ready"), sem("m_lo_ready")
        x2_in, x2_ready, x2_T, x2_hi_ready, x2_lo_ready = (sem(n) for n in (
            "x2_in", "x2_ready", "x2_T", "x2_hi_ready", "x2_lo_ready"))
        x2_ss, x2_rstd, diag_ready, rstd_T, rstd_b_ready = (sem(n) for n in (
            "x2_ss", "x2_rstd", "diag_ready", "rstd_T", "rstd_b_ready"))
        gate_f_scaled, gate_f_ready, a_ready, a_hi_ready, a_lo_ready = (sem(n) for n in (
            "gate_f_scaled", "gate_f_ready", "a_ready", "a_hi_ready", "a_lo_ready"))
        out_ready, out_done = sem("out_ready"), [sem(f"out_done{p}") for p in range(2)]

        block = ctx.enter_context(nc.Block())

        conv_rows = conv_w[0].rearrange("j (m p) -> (j m) p", p=P)

        @block.sync
        def _(sp):
            unit = Tally()

            def load(source, row_tile, col):
                s = unit.n
                if not (unit.n < RING and isinstance(unit.base, int)):
                    sp.wait_ge(lo_ready, unit.now(1 - RING))
                src = source[0, row_tile * P:(row_tile + UK) * P, bass.ds(col, CW)]
                sp.dma_start(w_raw[:, s % RING], src.rearrange("(k p) n -> p k n", p=P)).then_inc(raw_in[s % RING], 16)
                unit.step()

            def chunk(source, col, units=UPC):
                for u in range(units):
                    load(source, u * UK, col)

            for t in range(TT):
                sp.dma_start(x_row[:, t], x[0, t * P:(t + 1) * P, :]).then_inc(x_in[t], 16)
            for j in range(2):
                sp.dma_start(rows[0:R_CONV, j], conv_rows[j * R_CONV:(j + 1) * R_CONV, :]).then_inc(rows_in, 16)
            for first, last, vector in ((R_BIAS, R_MIX, conv_b), (R_MIX, R_FFN, mix_norm_w), (R_FFN, R_SSM, ffn_norm_w),
                                        (R_SSM, R_SUB, ssm_norm_w), (R_SUB, R_ALL, subln_w)):
                sp.dma_start(rows[first:last, 2], vector[0].rearrange("(m p) -> m p", p=P)).then_inc(rows_in, 16)
            for c in range(4):
                for u in range(UPC):
                    load(w_in, u * UK, COL_Q + c * CW)
                    if c == 0 and u == RING - 1:
                        vectors = (dt_bias, a_log, d_skip, q_norm_w, k_norm_w, lambda_q1, lambda_k1, lambda_q2, lambda_k2)
                        for n, vector in enumerate(vectors):
                            sp.dma_start(bcast[:, n], vector[0].partition_broadcast(P)).then_inc(bcast_in, 16)
                        sp.dma_start(rope_in[:], consts[:, C_ROPE:].rearrange("p (t w d) -> p t w d", t=TT, w=2)).then_inc(tables_in, 16)
                        sp.dma_start(mask_in[:], consts[:, C_MASK_QK:C_MASK_QK + P]).then_inc(tables_in, 16)
            for first, pairs in ((COL_K, 2), (COL_V, 2)):
                with repeat(sp, pairs, [(unit, 2 * UPC)]) as i:
                    for c in range(2):
                        chunk(w_in, i * (2 * CW) + first + c * CW)
            sp.wait_ge(qk_ready, 2 * D // CW)
            sp.dma_start(wdt[:], w_in[0, :, COL_DT:COL_DT + HS].rearrange("(k p) n -> p k n", p=P)).then_inc(wdt_in, 16)
            for n, first in enumerate((COL_BC, COL_GA)):
                with repeat(sp, 2, [(unit, 2 * UPC)]) as i:
                    for c in range(2):
                        for u in range(UPC):
                            if u in (4, 5):
                                a = u - 4
                                head = 8 * n + 2 * c + a
                                sp.wait_ge(qk_T, i * 4 + max(head - 1, 0) + STARTED)
                                src = qk[:, :, bass.ds(i * 4 + head, 1)].rearrange("p w o t d -> p w (o t) d")
                                sp.dma_start(qk_row[:, a], src).then_inc(row_in[a], 16)
                            load(w_in, u * UK, i * (2 * CW) + first + c * CW)
            with repeat(sp, 2, [(unit, 2 * UPC)]) as i:
                for c in range(2):
                    chunk(w_attn_proj, i * (2 * CW) + c * CW)
            with repeat(sp, G, [(unit, 2 * UPC)]) as i:
                chunk(w_in, i * CW + COL_X)
                chunk(w_in, (i + i) * (CW // 2) + COL_Z)
            with repeat(sp, 2, [(unit, 2 * UPC)]) as i:
                for c in range(2):
                    chunk(w_in, i * (2 * CW) + COL_GS + c * CW)
            sp.wait_ge(y_T, G)
            sp.dma_start(x2[:], x[0].rearrange("(t p) d -> p t d", p=P)).then_inc(x2_in, 16)
            with repeat(sp, 2, [(unit, 4 * UPC)]) as i:
                for c in range(2):
                    chunk(w_ssm_proj, i * (2 * CW) + c * CW, 2 * UPC)
            with repeat(sp, 2, [(unit, 2 * UPC)]) as i:
                for c in range(2):
                    chunk(w_out, i * (2 * CW) + c * CW)
            with repeat(sp, FF // CW, [(unit, 2 * UPC)]) as i:
                chunk(w_ffn_gate, i * CW)
                chunk(w_ffn_up, i * CW)

            def store(c):
                for t in range(TT):
                    sp.wait_ge(out_ready, TT * c + t + 1)
                    sp.dma_start(out[0, t * P:(t + 1) * P, c * CW:(c + 1) * CW], out_row[:, c % 2, t]).then_inc(out_done[c % 2], 16)

            for c in range(D // CW):
                for u in range(KF // UK):
                    load(w_ffn_down, u * UK, c * CW)
                    if c and u == KF // UK // 2:
                        store(c - 1)
            store(D // CW - 1)
            for p in range(2):
                sp.wait_ge(out_done[p], 16 * TT * D // CW // 2)

        @block.scalar
        def _(act):
            unit = Tally()
            nc.scalar.dma_start(cst[:], consts[:, :3 * P]).then_inc(const_in, 16)
            for stage in (qk_T, scores, prob_ready, wts_ready, wts_T, pv, o_sums, o_T, ya_lo_ready):
                nc.scalar.sem_inc(stage, STARTED)
            nc.scalar.sem_inc(acc_free[0], 1)
            nc.scalar.sem_inc(acc_free[1], 1)

            def split_hi():
                s, r = unit.n, unit.n % RING
                act.wait_ge(raw_in[r], unit.base * (16 // RING) + 16 * (s // RING + 1))
                if not (isinstance(unit.base, int) and s < RING):
                    act.wait_ge(mm_done, unit.now(1 - RING))
                nc.scalar.activation(w_hi[:, r], w_raw[:, r], ACT.Copy).then_inc(hi_ready, 1)
                unit.step()

            def chunk_done():
                act.wait_ge(mm_done, unit.now(-LEAD))

            def sums(p):
                return acc[p][:].rearrange("p b (n t) -> p (b n) t", t=T)

            for t in range(TT):
                act.wait_ge(x_in[t], 16)
                nc.scalar.activation(qk[:, 0, 8 * t:8 * t + 8], x_row[:, t].rearrange("p (a b c) -> p a b c", a=8, b=2),
                                     ACT.Square, accum_out=x_ss[:, t:t + 1]).then_inc(ss_ready, 1)
            act.wait_ge(rows_T, 1)
            nc.scalar.activation(taps[:].rearrange("p j m -> p (j m)"), acc[1][:, 0, 0:2 * R_CONV], ACT.Copy).then_inc(cols_ready, 1)
            nc.scalar.activation(cols[:, 0:R_ALL], acc[1][:, 0, 2 * R_CONV:2 * R_CONV + R_ALL], ACT.Copy).then_inc(cols_ready, 1)
            act.wait_ge(cols_ready, 2)

            def h_rounded(b):
                act.wait_ge(side_T, b + 1)
                for k in (2 * b, 2 * b + 1):
                    last = nc.scalar.activation(h_hi[:, k], side[:, b % 4, (k % 2) * T:(k % 2 + 1) * T], ACT.Copy,
                                                scale=cols[:, R_MIX + k:R_MIX + k + 1])
                last.then_inc(side_hi, 1)

            for b in range(LEAD):
                h_rounded(b)
                split_hi()

            def chunk_squares(c, head):
                for u in range(UPC):
                    split_hi()
                    if head and LEAD + u < KD // 2:
                        h_rounded(LEAD + u)
                    if head and u == LEAD:
                        act.wait_ge(bcast_in, 9 * 16)
                        nc.scalar.activation(decay_rate[:], bcast[:, 1], ACT.Exp).then_inc(lam_exps, 1)
                        act.wait_ge(lam_sums, 2)
                        nc.scalar.activation(lam_parts, lam_dots, ACT.Exp).then_inc(lam_exps, 1)
                chunk_done()
                nc.scalar.activation(sq[:], acc[c][:], ACT.Square).then_inc(sq_read, 1)

            chunk_squares(0, True)
            chunk_squares(1, False)
            with repeat(act, 3, [(unit, 2 * UPC)]) as i:
                for c in range(2):
                    chunk_squares(c, False)
            with repeat(act, 2, [(unit, 2 * UPC)]) as i:
                for c in range(2):
                    for u in range(UPC):
                        split_hi()
                    chunk_done()
                    nc.scalar.activation(v_all[:, :, bass.ds(i * (2 * CW) + c * CW, CW)], acc[c][:], ACT.Copy).then_inc(acc_free[c], 1)

            def conv_first_taps(source, tile, buf, n):
                return nc.scalar.activation(buf, source, ACT.Identity, bias=cols[:, bass.ds(tile + (R_BIAS + n), 1)],
                                            scale=taps[:, TAPS - 1, bass.ds(tile + n, 1)])

            def qk_transposed(h):
                act.wait_ge(qk_T, h + 1 + STARTED)
                act.wait_ge(scores, h + STARTED)
                nc.scalar.activation(qkT[:].rearrange("p w t -> p (w t)"), side[:, 0, :], ACT.Copy).then_inc(qkT_ready, 1)

            def head_exps(h, b):
                act.wait_ge(max_ready, h + 1)
                act.wait_ge(wts_ready, h + STARTED)
                for q in range(TT):
                    cut = slice(0, P) if q == 0 else slice(P, 3 * P)
                    for m in range(2):
                        n = ATT_COLUMNS * b + 2 * q + m
                        last = nc.scalar.activation(prob[:, m, cut], side[:, 1 + m, cut], ACT.Exp, bias=att[:, n + MAX:n + MAX + 1],
                                                    accum_out=att[:, n + SUM:n + SUM + 1])
                last.then_inc(prob_ready, 1)

            def weights_transposed(h):
                act.wait_ge(wts_T, h + 1 + STARTED)
                act.wait_ge(pv, h + STARTED)
                nc.scalar.activation(wtsT[:], side[:, 0, 0:3 * P], ACT.Copy).then_inc(wtsT_ready, 1)

            def output_hi(h):
                act.wait_ge(o_T, h + 1 + STARTED)
                nc.scalar.activation(ya_hi[:, bass.ds(h, 1)].rearrange("p o t -> p (o t)"), side[:, 0, 0:T], ACT.Copy,
                                     scale=subln_scale).then_inc(ya_hi_ready, 1)

            def chunk_with_heads(a):
                for u in range(UPC):
                    split_hi()
                    if u == 0:
                        qk_transposed(a)
                    if u == 1:
                        qk_transposed(a + 1)
                        head_exps(a, 0)
                    if u == 2:
                        head_exps(a + 1, 1)
                    if u in (3, 4):
                        weights_transposed(a + (u - 3))
                    if u >= 6:
                        output_hi(a + (u - 6))
                chunk_done()

            with repeat(act, 2, [(unit, 2 * UPC)]) as i:
                for c in range(2):
                    chunk_with_heads(i * 4 + 2 * c)
                    nc.scalar.activation(bc_raw[:, bass.ds(i * (2 * CT) + c * CT, CT)], sums(c), ACT.Copy).then_inc(acc_free[c], 1)
            act.wait_ge(wdt_in, 16)
            nc.scalar.activation(wdt_hi[:], wdt[:], ACT.Copy).then_inc(wdt_hi_ready, 1)
            with repeat(act, 2, [(unit, 2 * UPC)]) as i:
                for c in range(2):
                    chunk_with_heads(i * 4 + (8 + 2 * c))
                    nc.scalar.activation(merge_a[:, bass.ds(i * (2 * CT) + c * CT, CT)], sums(c), ACT.Sigmoid).then_inc(acc_free[c], 1)
            act.wait_ge(dtT_sum, 1)
            nc.scalar.activation(dtT[:], side[0:HS, 1, 0:T], ACT.Copy).then_inc(dtT_ready, 1)
            act.wait_ge(dt_u, 1)
            nc.scalar.activation(soft[:, 2], soft[:, 1], ACT.Exp).then_inc(dt_exp, 1)
            act.wait_ge(pv, NA + STARTED)
            with repeat(act, 2, [(unit, 2 * UPC)]) as i:
                for c in range(2):
                    for u in range(UPC):
                        split_hi()
                        if u == 0:
                            first = i * (2 * CT) + c * CT
                            for n in range(CT):
                                last = conv_first_taps(bc_raw[:, bass.ds(first + n, 1)], first + DI // P,
                                                       bc[:, bass.ds(first + n, 1)], n)
                            last.then_inc(bc_first, 1)

            act.wait_ge(acs_sum, 1)
            nc.scalar.activation(neg_acs[:].rearrange("p t h -> p (t h)"), side[:, 1, 0:TT * HS], ACT.Copy, scale=-1.0).then_inc(acs_ready, 1)
            nc.scalar.activation(acsT[:], side[0:HS, 2, 0:T], ACT.Copy).then_inc(acs_ready, 1)
            act.wait_ge(acs_ready, 2)

            def tail_squares(g):
                act.wait_ge(y_gated, g + 1)
                for t in range(TT):
                    last = nc.scalar.activation(z_row[:, t], y_row[:, t], ACT.Square, accum_out=y_ss[:, t:t + 1])
                last.then_inc(y_squared, 1)

            def x_chunk(g, head):
                for u in range(UPC):
                    split_hi()
                    if head and u < 2 * G // CT:
                        act.wait_ge(bc_conv, u + 1)
                        ours = bc[:, u * CT:(u + 1) * CT]
                        nc.scalar.activation(ours, ours, ACT.Silu).then_inc(bc_ready, 1)
                    if head and u == 4:
                        nc.scalar.activation(edge[:].rearrange("p t h -> p (t h)"), side[:, 3, 0:TT * HS], ACT.Exp).then_inc(edge_ready, 1)
                    if u == 4 and not head:
                        tail_squares(g - 1)
                    if u == 6:
                        if head:
                            act.wait_ge(bc_ready, 2 * G // CT)
                        else:
                            act.wait_ge(cb_sum, g)
                        nc.scalar.activation(bT[:], bc[:, bass.ds(g, 1)].rearrange("p o t -> p (o t)"), ACT.Copy).then_inc(bT_ready, 1)
                chunk_done()
                for n in range(CT):
                    last = conv_first_taps(sums(0)[:, n], g * CT, conv_x[:, n], n)
                    if n % 2:
                        last.then_inc(conv_first, 1)

            def exps(g, hf, head):
                act.wait_ge(acs_masked, g * 2 + (hf + 1))
                if hf == 0 and not head:
                    act.wait_ge(y_sum, g)
                for h4 in range(HG // 2):
                    h = hf * (HG // 2) + h4
                    for t in range(TT):
                        last = nc.scalar.activation(decay[:, h, t], acs_b[:, hf, h4, t * P:(t + 1) * P], ACT.Exp,
                                                    bias=neg_acs[:, t, bass.ds(g * HG + h, 1)])
                last.then_inc(decay_exp, 1)

            def z_chunk(g, head):
                for u in range(UPC):
                    split_hi()
                    if u == 1:
                        act.wait_ge(cb_sum, g + 1)
                        nc.scalar.activation(cb[:], side[:, 0, 0:3 * P], ACT.Copy).then_inc(cb_ready, 1)
                        act.wait_ge(conv_done, g + 1)
                        nc.scalar.activation(conv_x[:], conv_x[:], ACT.Silu).then_inc(xs_ready, 1)
                    if u == 2:
                        exps(g, 0, head)
                    if u == 3:
                        exps(g, 1, head)
                    if u == 4:
                        act.wait_ge(xdt_ready, g + 1)
                        nc.scalar.activation(y_row[:], side[:, 2:4], ACT.Copy).then_inc(xrow_ready, 1)
                chunk_done()
                nc.scalar.activation(z_row[:], acc[1][:], ACT.Silu).then_inc(z_ready, 1)
                act.wait_ge(z_ready, g + 1)
                nc.scalar.sem_inc(acc_free[1], 1)

            x_chunk(0, True)
            z_chunk(0, True)
            with repeat(act, G - 1, [(unit, 2 * UPC)]) as i:
                x_chunk(i + 1, False)
                z_chunk(i + 1, False)

            for c in range(4):
                for u in range(UPC):
                    split_hi()
                    if c == 0 and u == 4:
                        tail_squares(G - 1)
                    if c >= 1 and u in (1, 3, 5):
                        n = 3 * (c - 1) + (u - 1) // 2
                        if n < KI // 4:
                            act.wait_ge(yT_ready, G)
                            nc.scalar.activation(y_hi[:, 4 * n:4 * n + 4], yT[:, 4 * n:4 * n + 4], ACT.Copy).then_inc(y_hi_ready, 1)
                chunk_done()
                nc.scalar.activation(gate_s[:, c * CT:(c + 1) * CT], sums(c % 2), ACT.Sigmoid).then_inc(acc_free[c % 2], 1)

            with repeat(act, 2, [(unit, 4 * UPC)]) as i:
                for c in range(2):
                    for u in range(2 * UPC):
                        split_hi()
                    act.wait_ge(m_ready, i * 2 + c + 1)
                    nc.scalar.activation(m_hi[:, bass.ds(i * (2 * CT) + c * CT, CT)], m_row[:], ACT.Copy).then_inc(m_hi_ready, 1)

            def residual_hi(c):
                act.wait_ge(x2_T, c + 1)
                for n in range(CT):
                    k = c * CT + n
                    last = nc.scalar.activation(x2T_hi[:, k], side[:, 2:4].rearrange("p b (n t) -> p (b n) t", t=T)[:, n],
                                                ACT.Copy, scale=cols[:, R_FFN + k:R_FFN + k + 1])
                last.then_inc(x2_hi_ready, 1)

            for c in range(4):
                for u in range(UPC):
                    split_hi()
                    if c and u == 3:
                        residual_hi(c - 1)

            def gate_silu(i):
                act.wait_ge(gate_f_scaled, i + 1)
                nc.scalar.activation(gate_f[:], gate_f[:], ACT.Silu).then_inc(gate_f_ready, 1)

            def up_hi(i):
                act.wait_ge(a_ready, i + 1)
                nc.scalar.activation(a_hi[:, bass.ds(i * CT, CT)], up_f[:], ACT.Copy).then_inc(a_hi_ready, 1)

            def ffn_pair(i, head):
                for u in range(UPC):
                    split_hi()
                    if head and u == 2:
                        residual_hi(3)
                    if head and u in (3, 4):
                        t = u - 3
                        nc.scalar.activation(x2_sq[:, t], x2[:, t], ACT.Square, accum_out=x2_sums[:, t:t + 1]).then_inc(x2_ss, 1)
                    if head and u == 7:
                        act.wait_ge(rstd_T, 1)
                        nc.scalar.activation(rstd_b[:], side[:, 0, 0:T], ACT.Copy).then_inc(rstd_b_ready, 1)
                for u in range(UPC):
                    split_hi()
                    if u == 1:
                        gate_silu(i)
                up_hi(i)

            ffn_pair(0, True)
            with repeat(act, FF // CW - 1, [(unit, 2 * UPC)]) as i:
                ffn_pair(i + 1, False)

            for _ in range(4 * (KF // UK) - LEAD):
                split_hi()

        @block.vector
        def _(dve):
            unit, own = Tally(), Tally()

            def link(instruction):
                instruction.then_inc(dve_step, 1)
                dve.wait_ge(dve_step, own.step())

            def split_lo():
                r = unit.n % RING
                dve.wait_ge(hi_ready, unit.now(1))
                nc.vector.tensor_tensor(w_lo[:, r], w_raw[:, r], w_hi[:, r].bitcast(F32), ALU.subtract).then_inc(lo_ready, 1)
                unit.step()

            def chunk_done():
                dve.wait_ge(mm_done, unit.now(-LEAD))

            def sums(p):
                return acc[p][:].rearrange("p b (n t) -> p (b n) t", t=T)

            nc.vector.memset(ones[:], 1.0).then_inc(ones_ready, 1)
            for t in range(TT):
                dve.wait_ge(rstd_ready, t + 1)
                for half in ((slice(0, D),) if t == 0 else (slice(0, D // 2), slice(D // 2, D))):
                    nc.vector.tensor_scalar(x_row[:, t, half], x_row[:, t, half], x_rstd[:, t:t + 1], None, ALU.mult).then_inc(x_normed, 1)
            dve.wait_ge(cols_ready, 2)
            def h_remainder(b):
                dve.wait_ge(side_hi, b + 1)
                for k in (2 * b, 2 * b + 1):
                    last = nc.vector.scalar_tensor_tensor(
                        out=h_lo[:, k], in0=side[:, b % 4, (k % 2) * T:(k % 2 + 1) * T], scalar=cols[:, R_MIX + k:R_MIX + k + 1],
                        in1=h_hi[:, k].bitcast(F32), op0=ALU.mult, op1=ALU.subtract)
                last.then_inc(side_lo, 1)

            for b in range(LEAD):
                h_remainder(b)
                split_lo()

            def tables_and_lambda():
                dve.wait_ge(bcast_in, 9 * 16)
                dve.wait_ge(tables_in, 32)
                dve.wait_ge(const_in, 16)
                nc.vector.tensor_copy(ident_b[:], ident)
                nc.vector.tensor_copy(mask_b[:], mask_in[:]).then_inc(setup_done, 1)
                for n in range(2):
                    nc.vector.tensor_tensor_reduce(out=o_sq[:, n, 0:DH], in0=bcast[:, 5 + 2 * n], in1=bcast[:, 6 + 2 * n], scale=1.0,
                                                   scalar=0.0, op0=ALU.mult, op1=ALU.add,
                                                   accum_out=lam_dots[:, n:n + 1]).then_inc(lam_sums, 1)
                nc.vector.tensor_copy(dt_bias_b[:], bcast[:, 0])
                nc.vector.tensor_copy(d_skip_b[:], bcast[:, 2])
                for w in range(2):
                    norm_w = bcast[:, 3 + w]
                    scale = DH ** -0.5 if w == 0 else 1.0
                    half = DH // 2
                    for t in range(TT):
                        nc.vector.scalar_tensor_tensor(out=rope[:, w, t, 0], in0=rope_in[:, t, 0], scalar=scale, in1=norm_w,
                                                       op0=ALU.mult, op1=ALU.mult)
                        for first, other in ((0, half), (half, 0)):
                            last = nc.vector.scalar_tensor_tensor(
                                out=rope[:, w, t, 1, first:first + half], in0=rope_in[:, t, 1, first:first + half], scalar=scale,
                                in1=norm_w[:, other:other + half], op0=ALU.mult, op1=ALU.mult)
                link(last)
                dve.wait_ge(lam_exps, 2)
                link(nc.vector.tensor_tensor(minus_lam, lam_parts[:, 1:2], lam_parts[:, 0:1], ALU.subtract))
                link(nc.vector.tensor_scalar(minus_lam, minus_lam, -LAM_INIT, None, ALU.add))
                dve.wait_ge(cols_ready, 2)
                link(nc.vector.tensor_scalar(subln_scale, cols[:, R_SUB:R_SUB + 1], 1.0 - LAM_INIT, None, ALU.mult))

            half = DH // 2

            def per_head(tile):
                return tile.rearrange("p t (h d) -> p t h d", d=DH)

            def qk_chunk(which, i, c, head=False):
                for u in range(UPC):
                    split_lo()
                    if head and LEAD + u < KD // 2:
                        h_remainder(LEAD + u)
                    if head and u == LEAD:
                        tables_and_lambda()
                dve.wait_ge(sq_read, i * 2 + (4 * which + c + 1))
                nc.vector.tensor_reduce(out=qk_ss, in_=sq[:].rearrange("p t (h d) -> p (t h) d", d=DH),
                                        op=ALU.add, axis=AX).then_inc(ss_ready, 1)
                heads, main, swapped = per_head(acc[c][:]), per_head(rot_a[:]), per_head(rot_b[:])
                shape = [P, TT, CW // DH, DH]
                nc.vector.tensor_tensor(main, heads, rope[:, which, :, 0:1].broadcast_to(shape), ALU.mult)
                shape = [P, TT, CW // DH, half]
                nc.vector.tensor_tensor(swapped[..., 0:half], heads[..., half:DH],
                                        rope[:, which, :, 1:2, 0:half].broadcast_to(shape), ALU.mult)
                nc.vector.tensor_tensor(swapped[..., half:DH], heads[..., 0:half],
                                        rope[:, which, :, 1:2, half:DH].broadcast_to(shape), ALU.mult).then_inc(acc_free[c], 1)
                dve.wait_ge(acc_free[c], i + (2 + 2 * which))
                link(nc.vector.tensor_tensor(rot_a[:], rot_a[:], rot_b[:], ALU.add))
                dve.wait_ge(rstd_ready, i * 2 + (2 + 4 * which + c + 1))
                for t in range(TT):
                    src = rot_a[:, t].rearrange("p (n s d) -> p n s d", s=2, d=DH)
                    dst = qk[:, which, bass.ds(i * 8 + c * 4, 4), t].rearrange("p n (s d) -> p n s d", d=DH)
                    rstd = qk_rstd[:, 8 * t:8 * t + 8].rearrange("p (n s) -> p n s", s=2).unsqueeze(3)
                    last = nc.vector.tensor_tensor(dst, src, rstd.broadcast_to([P, 4, 2, DH]), ALU.mult)
                last.then_inc(qk_ready, 1)

            for i in range(2):
                for c in range(2):
                    qk_chunk(0, i, c, head=i == c == 0)
            with repeat(dve, 2, [(unit, 2 * UPC), (own, 2)]) as i:
                for c in range(2):
                    qk_chunk(1, i, c)
            with repeat(dve, 2, [(unit, 2 * UPC)]) as i:
                for c in range(2):
                    for u in range(UPC):
                        split_lo()

            def conv_other_taps(source, tile, buf, n, back):
                return nc.vector.scalar_tensor_tensor(
                    out=buf[:, back:T], in0=source[:, 0:T - back], scalar=taps[:, TAPS - 1 - back, bass.ds(tile + n, 1)],
                    in1=buf[:, back:T], op0=ALU.mult, op1=ALU.add)

            def row_maxes(h, b):
                dve.wait_ge(scores, h + 1 + STARTED)
                n = ATT_COLUMNS * b
                nc.vector.tensor_reduce(out=att[:, n + MAX:n + MAX + 2], in_=side[:, 1:3, 0:P], op=ALU.max, axis=AX, negate=True)
                nc.vector.tensor_reduce(out=att[:, n + MAX + 2:n + MAX + 4], in_=side[:, 1:3, P:3 * P], op=ALU.max, axis=AX,
                                        negate=True).then_inc(max_ready, 1)

            def weights(h, b):
                dve.wait_ge(prob_ready, h + 1 + STARTED)
                dve.wait_ge(wts_T, h + STARTED)
                n = ATT_COLUMNS * b
                link(nc.vector.reciprocal(att[:, n + INVERSE:n + INVERSE + 4], att[:, n + SUM:n + SUM + 4]))
                total = att[:, n + SUM:n + SUM + 4].rearrange("p (q m) -> p q m", m=2)
                inverse = att[:, n + INVERSE:n + INVERSE + 4].rearrange("p (q m) -> p q m", m=2)
                link(nc.vector.scalar_tensor_tensor(out=att[:, n + RATIO:n + RATIO + 2], in0=inverse[:, :, 1], scalar=minus_lam,
                                                    in1=total[:, :, 0], op0=ALU.mult, op1=ALU.mult))
                for q in range(TT):
                    cut = slice(0, P) if q == 0 else slice(P, 3 * P)
                    last = nc.vector.scalar_tensor_tensor(out=wts[:, cut], in0=prob[:, 1, cut], scalar=att[:, n + RATIO + q:n + RATIO + q + 1],
                                                          in1=prob[:, 0, cut], op0=ALU.mult, op1=ALU.add)
                last.then_inc(wts_ready, 1)

            def head_output(h, b):
                dve.wait_ge(pv, h + 1 + STARTED)
                dve.wait_ge(o_T, h + (STARTED - 1))
                n = ATT_COLUMNS * b
                for q in range(TT):
                    last = nc.vector.tensor_scalar(o_row[:, b, q], side[:, 3, q * P:(q + 1) * P], att[:, n + INVERSE + 2 * q:n + INVERSE + 2 * q + 1],
                                                   None, ALU.mult)
                link(last)
                for q in range(TT):
                    last = nc.vector.tensor_tensor_reduce(out=o_sq[:, q], in0=o_row[:, b, q], in1=o_row[:, b, q], scale=1.0, scalar=0.0,
                                                          op0=ALU.mult, op1=ALU.add, accum_out=att[:, n + SQUARES + q:n + SQUARES + q + 1])
                last.then_inc(o_sums, 1)

            def head_normed(h, b):
                dve.wait_ge(o_rstd, h + 1)
                for q in range(TT):
                    n = ATT_COLUMNS * b + RSTD + q
                    last = nc.vector.tensor_scalar(o_row[:, b, q], o_row[:, b, q], att[:, n:n + 1], None, ALU.mult)
                last.then_inc(o_ready, 1)

            def output_lo(h):
                dve.wait_ge(ya_hi_ready, h + 1)
                nc.vector.scalar_tensor_tensor(
                    out=ya_lo[:, bass.ds(h, 1)].rearrange("p o t -> p (o t)"), in0=side[:, 0, 0:T], scalar=subln_scale,
                    in1=ya_hi[:, bass.ds(h, 1)].rearrange("p o t -> p (o t)").bitcast(F32),
                    op0=ALU.mult, op1=ALU.subtract).then_inc(ya_lo_ready, 1)

            def chunk_with_heads(a):
                for u in range(UPC):
                    if u == 1:
                        row_maxes(a, 0)
                    if u == 2:
                        weights(a, 0)
                        row_maxes(a + 1, 1)
                    if u == 3:
                        weights(a + 1, 1)
                    if u == 6:
                        output_lo(a)
                        head_normed(a + 1, 1)
                    split_lo()
                    if u == 4:
                        head_output(a, 0)
                    if u == 5:
                        head_normed(a, 0)
                        head_output(a + 1, 1)
                    if u == 7:
                        output_lo(a + 1)

            head_links = 2 * (2 + 1)
            conv_links = 2 * (TAPS - 2)

            with repeat(dve, 2, [(unit, 2 * UPC), (own, 2 * head_links)]) as i:
                for c in range(2):
                    chunk_with_heads(i * 4 + 2 * c)
            dve.wait_ge(wdt_hi_ready, 1)
            nc.vector.tensor_tensor(wdt_lo[:], wdt[:], wdt_hi[:].bitcast(F32), ALU.subtract).then_inc(wdt_ready, 1)
            with repeat(dve, 2, [(unit, 2 * UPC), (own, 2 * head_links)]) as i:
                for c in range(2):
                    chunk_with_heads(i * 4 + (8 + 2 * c))
            def steps_of_dt():
                v, mag, u, p, s, s2 = (soft[:, n] for n in range(6))
                by_tile = "p (t h) -> p t h"
                dve.wait_ge(dt_sum, 1)
                link(nc.vector.tensor_tensor(v.rearrange(by_tile, h=HS), side[:, 2, 0:TT * HS].rearrange(by_tile, h=HS),
                                             dt_bias_b[:].unsqueeze(1).broadcast_to([P, TT, HS]), ALU.add))
                nc.vector.scalar_tensor_tensor(out=mag, in0=v, scalar=-1.0, in1=v, op0=ALU.mult, op1=ALU.min).then_inc(dt_u, 1)
                dve.wait_ge(dt_exp, 1)
                link(nc.vector.tensor_scalar(p, u, 2.0, None, ALU.add))
                link(nc.vector.reciprocal(p, p))
                link(nc.vector.tensor_tensor(s, u, p, ALU.mult))
                link(nc.vector.tensor_tensor(s2, s, s, ALU.mult))
                link(nc.vector.tensor_scalar(p, s2, 1.0 / 15, None, ALU.mult))
                for odd in (13, 11, 9, 7, 5, 3):
                    link(nc.vector.scalar_tensor_tensor(out=p, in0=p, scalar=1.0 / odd, in1=s2, op0=ALU.add, op1=ALU.mult))
                link(nc.vector.scalar_tensor_tensor(out=p, in0=p, scalar=1.0, in1=s, op0=ALU.add, op1=ALU.mult))
                link(nc.vector.tensor_scalar(mag, v, 0.0, None, ALU.max))
                link(nc.vector.scalar_tensor_tensor(out=dt[:].rearrange("p t h -> p (t h)"), in0=p, scalar=2.0, in1=mag,
                                                    op0=ALU.mult, op1=ALU.add))
                nc.vector.scalar_tensor_tensor(out=dA[:], in0=dt[:], scalar=-1.0,
                                               in1=decay_rate[:].unsqueeze(1).broadcast_to([P, TT, HS]),
                                               op0=ALU.mult, op1=ALU.mult).then_inc(dA_ready, 1)

            steps_of_dt()
            nc.vector.tensor_tensor(after[:], ones[:], tri, ALU.subtract).then_inc(after_ready, 1)
            with repeat(dve, 2, [(unit, 2 * UPC), (own, 2 * (TAPS - 2))]) as i:
                for c in range(2):
                    for u in range(UPC):
                        split_lo()
                        if 1 <= u < TAPS:
                            if u == 1:
                                dve.wait_ge(bc_first, i * 2 + (c + 1))
                            first = i * (2 * CT) + c * CT
                            for n in range(CT):
                                last = conv_other_taps(bc_raw[:, bass.ds(first + n, 1)].rearrange("p o t -> p (o t)"), first + DI // P,
                                                       bc[:, bass.ds(first + n, 1)].rearrange("p o t -> p (o t)"), n, u)
                            if u < TAPS - 1:
                                link(last)
                            else:
                                last.then_inc(bc_conv, 1)
                    chunk_done()
                    gated = merge_a[:, bass.ds(i * (2 * CT) + c * CT, CT)]
                    nc.vector.tensor_tensor(gated, sums(c), gated, ALU.mult).then_inc(acc_free[c], 1)

            def tail_gated(g):
                dve.wait_ge(y_sum, g + 1)
                by_head = "p (h d) -> p h d"
                nc.vector.tensor_tensor(
                    xdt_end[:].rearrange(by_head, d=HP), side[:, 2].rearrange(by_head, d=HP),
                    edge[:, 1, bass.ds(g * HG, HG)].unsqueeze(2).broadcast_to([P, HG, HP]), ALU.mult)
                dve.wait_ge(skip_ready, g + 1)
                nc.vector.tensor_tensor(y_row[:], side[:, 0:2], y_row[:], ALU.add).then_inc(y_added, 1)
                dve.wait_ge(y_added, g + 1)
                nc.vector.tensor_tensor(y_row[:, 1], xdt_end[:], y_row[:, 1], ALU.add).then_inc(late_ready, 1)
                dve.wait_ge(late_ready, g + 1)
                dve.wait_ge(z_ready, g + 1)
                nc.vector.tensor_tensor(y_row[:], y_row[:], z_row[:], ALU.mult).then_inc(y_gated, 1)

            def tail_normed(g):
                dve.wait_ge(y_rstd, g + 1)
                for t in range(TT):
                    last = nc.vector.tensor_scalar(y_row[:, t], y_row[:, t], y_scale[:, t:t + 1], None, ALU.mult)
                last.then_inc(y_ready, 1)

            def tail_transposed(g):
                dve.wait_ge(y_T, g + 1)
                nc.vector.tensor_tensor(yT[:, bass.ds(g * CT, CT)], side[:, 2:4].rearrange("p b (n t) -> p (b n) t", t=T),
                                        cols[:, bass.ds(g * CT + R_SSM, CT)].unsqueeze(2).broadcast_to([P, CT, T]),
                                        ALU.mult).then_inc(yT_ready, 1)

            def x_chunk(g, head):
                for u in range(UPC):
                    split_lo()
                    if not head:
                        if u == 3:
                            tail_gated(g - 1)
                        if u == 6:
                            tail_normed(g - 1)
                for b in range(2):
                    dve.wait_ge(conv_first, g * 2 + (b + 1))
                    for back in range(1, TAPS):
                        for n in (2 * b, 2 * b + 1):
                            last = conv_other_taps(sums(0)[:, n], g * CT, conv_x[:, n], n, back)
                        if back < TAPS - 1:
                            link(last)
                last.then_inc(conv_done, 1)
                dve.wait_ge(conv_done, g + 1)
                nc.vector.sem_inc(acc_free[0], 1)

            def decays(g, hf):
                dve.wait_ge(decay_exp, g * 2 + (hf + 1))
                if hf == 0:
                    dve.wait_ge(cb_ready, g + 1)
                heads = decay[:, hf * 4:hf * 4 + 4]
                blocks = cb[:].rearrange("p (n l) -> p n l", l=P)[:, 0:3:2].unsqueeze(1).broadcast_to([P, HG // 2, TT, P])
                nc.vector.tensor_tensor(heads, heads, blocks, ALU.mult).then_inc(decay_ready, 1)

            def z_chunk(g, head):
                by_head = "p (h d) -> p h d"
                for u in range(UPC):
                    split_lo()
                    if u == 1 and not head:
                        tail_transposed(g - 1)
                    if u == 3:
                        decays(g, 0)
                    if u == 4:
                        dve.wait_ge(xs_T, g + 1)
                        for t in range(TT):
                            last = nc.vector.tensor_tensor(
                                xdt[:, t].rearrange(by_head, d=HP), side[:, 2 + t].rearrange(by_head, d=HP),
                                dt[:, t, bass.ds(g * HG, HG)].unsqueeze(2).broadcast_to([P, HG, HP]), ALU.mult)
                        last.then_inc(xdt_ready, 1)
                        dve.wait_ge(xdt_ready, g + 1)
                        if head:
                            dve.wait_ge(edge_ready, 1)
                        nc.vector.tensor_tensor(
                            xdt_end[:].rearrange(by_head, d=HP), xdt[:, 0].rearrange(by_head, d=HP),
                            edge[:, 0, bass.ds(g * HG, HG)].unsqueeze(2).broadcast_to([P, HG, HP]), ALU.mult).then_inc(xdt_end_ready, 1)
                    if u == 5:
                        decays(g, 1)

            x_chunk(0, True)
            z_chunk(0, True)
            with repeat(dve, G - 1, [(unit, 2 * UPC), (own, conv_links)]) as i:
                x_chunk(i + 1, False)
                z_chunk(i + 1, False)

            for c in range(4):
                for u in range(UPC):
                    split_lo()
                    if c == 0 and u == 3:
                        tail_gated(G - 1)
                    if c == 0 and u == 6:
                        tail_normed(G - 1)
                    if c == 1 and u == 1:
                        tail_transposed(G - 1)
                    if c and u in (1, 3, 5) and 3 * (c - 1) + u // 2 < KI // 4:
                        n = 3 * (c - 1) + u // 2
                        dve.wait_ge(y_hi_ready, n + 1)
                        cut = slice(4 * n, 4 * n + 4)
                        nc.vector.tensor_tensor(y_lo[:, cut], yT[:, cut], y_hi[:, cut].bitcast(F32), ALU.subtract).then_inc(y_lo_ready, 1)

            with repeat(dve, 2, [(unit, 4 * UPC), (own, 2)]) as i:
                for c in range(2):
                    for u in range(2 * UPC):
                        split_lo()
                    chunk_done()
                    cut = bass.ds(i * (2 * CT) + c * CT, CT)
                    link(nc.vector.tensor_tensor(m_row[:], sums(c), gate_s[:, cut], ALU.mult))
                    nc.vector.sem_inc(acc_free[c], 1)
                    nc.vector.tensor_tensor(m_row[:], m_row[:], merge_a[:, cut], ALU.add).then_inc(m_ready, 1)
                    dve.wait_ge(m_hi_ready, i * 2 + (c + 1))
                    nc.vector.tensor_tensor(m_lo[:, cut], m_row[:], m_hi[:, cut].bitcast(F32), ALU.subtract).then_inc(m_lo_ready, 1)

            def residual_lo(c):
                dve.wait_ge(x2_hi_ready, c + 1)
                for n in range(CT):
                    k = c * CT + n
                    last = nc.vector.scalar_tensor_tensor(
                        out=x2T_lo[:, k], in0=side[:, 2:4].rearrange("p b (n t) -> p (b n) t", t=T)[:, n],
                        scalar=cols[:, R_FFN + k:R_FFN + k + 1], in1=x2T_hi[:, k].bitcast(F32), op0=ALU.mult, op1=ALU.subtract)
                last.then_inc(x2_lo_ready, 1)

            dve.wait_ge(x2_in, 16)
            for c in range(D // CW):
                for u in range(UPC):
                    split_lo()
                    if c and u == 4:
                        residual_lo(c - 1)
                chunk_done()
                cut = slice(c * CW, (c + 1) * CW)
                nc.vector.tensor_tensor(x2[:, :, cut], acc[c % 2][:], x2[:, :, cut], ALU.add).then_inc(x2_ready, 1)
                dve.wait_ge(x2_ready, c + 1)
                nc.vector.sem_inc(acc_free[c % 2], 1)

            def ffn_pair(i, head):
                for u in range(UPC):
                    split_lo()
                    if head and u == 3:
                        residual_lo(D // CW - 1)
                    if head and u == 6:
                        dve.wait_ge(x2_rstd, 1)
                        for t in range(TT):
                            last = nc.vector.tensor_scalar(diag[:, t], ident, x2_scale[:, t:t + 1], None, ALU.mult)
                        last.then_inc(diag_ready, 1)
                if head:
                    dve.wait_ge(rstd_b_ready, 1)
                rstd = rstd_b[:].unsqueeze(1).broadcast_to([P, CT, T])
                chunk_done()
                nc.vector.tensor_tensor(gate_f[:], sums(0), rstd, ALU.mult).then_inc(gate_f_scaled, 1)
                dve.wait_ge(gate_f_scaled, i + 1)
                nc.vector.sem_inc(acc_free[0], 1)
                for u in range(UPC):
                    split_lo()
                chunk_done()
                link(nc.vector.tensor_tensor(up_f[:], sums(1), rstd, ALU.mult))
                nc.vector.sem_inc(acc_free[1], 1)
                dve.wait_ge(gate_f_ready, i + 1)
                nc.vector.tensor_tensor(up_f[:], up_f[:], gate_f[:], ALU.mult).then_inc(a_ready, 1)
                cut = bass.ds(i * CT, CT)
                dve.wait_ge(a_hi_ready, i + 1)
                nc.vector.tensor_tensor(a_lo[:, cut], up_f[:], a_hi[:, cut].bitcast(F32), ALU.subtract).then_inc(a_lo_ready, 1)

            ffn_pair(0, True)
            with repeat(dve, FF // CW - 1, [(unit, 2 * UPC), (own, 1)]) as i:
                ffn_pair(i + 1, False)

            for c in range(D // CW):
                final = c == D // CW - 1
                for u in range(KF // UK - (LEAD if final else 0)):
                    split_lo()
                dve.wait_ge(mm_done, unit.now(0 if final else -LEAD))
                if c >= 2:
                    dve.wait_ge(out_done[c % 2], 16 * TT)
                cut = slice(c * CW, (c + 1) * CW)
                for t in range(TT):
                    nc.vector.tensor_tensor(out_row[:, c % 2, t], acc[c % 2][:, t], x2[:, t, cut], ALU.add).then_inc(out_ready, 1)
                dve.wait_ge(out_ready, TT * (c + 1))
                nc.vector.sem_inc(acc_free[c % 2], 1)

        @block.gpsimd
        def _(pool):
            own = Tally()

            def rsqrt(out, mean_of, sums_at, tmp, eps):
                n = sums_at.shape[1]
                nc.gpsimd.tensor_tensor(tmp, sums_at, constant[1 / mean_of][:, 0:n], ALU.mult).then_inc(pool_step, 1)
                pool.wait_ge(pool_step, own.step())
                nc.gpsimd.tensor_tensor(tmp, tmp, constant[eps][:, 0:n], ALU.add).then_inc(pool_step, 1)
                pool.wait_ge(pool_step, own.step())
                return nc.gpsimd.tensor_tensor(out, tmp, power[:, 0:n], ALU.pow)

            constant = {}
            for n, value in enumerate((1 / D, 1 / DH, 1 / (2 * DH), 1 / CW, NORM_EPS, SUBLN_EPS)):
                constant[value] = pool_constants[:, n]
                nc.gpsimd.memset(constant[value], value)
            nc.gpsimd.memset(power, -0.5).then_inc(pool_step, 1)
            pool.wait_ge(pool_step, own.step())
            for t in range(TT):
                pool.wait_ge(ss_ready, t + 1)
                rsqrt(x_rstd[:, t:t + 1], D, x_ss[:, t:t + 1], x_scratch[:, t:t + 1], NORM_EPS).then_inc(rstd_ready, 1)
            with repeat(pool, 2 * D // CW, [(own, 2)]) as i:
                pool.wait_ge(ss_ready, i + (TT + 1))
                rsqrt(qk_rstd, DH, qk_ss, qk_scratch, NORM_EPS).then_inc(rstd_ready, 1)
            with repeat(pool, NA // 2, [(own, 4)]) as i:
                for b in range(2):
                    pool.wait_ge(o_sums, i * 2 + (b + 1) + STARTED)
                    n = ATT_COLUMNS * b
                    squares, scratch, rstd = (att[:, n + m:n + m + TT] for m in (SQUARES, SCRATCH, RSTD))
                    rsqrt(rstd, 2 * DH, squares, scratch, SUBLN_EPS).then_inc(o_rstd, 1)

            def tail(g):
                pool.wait_ge(y_squared, g + 1)
                rsqrt(y_scale, CW, y_ss, y_scratch, SUBLN_EPS).then_inc(y_rstd, 1)

            def loads(g):
                for hf in range(2):
                    heads = acs_dram[bass.ds(g * HG + hf * 4, 4), :]
                    pool.dma_start(acs_b[:, hf], heads.partition_broadcast(P)).then_inc(acs_in[hf], 16)

            def group(g):
                mask = mask_sl.unsqueeze(1).unsqueeze(1).broadcast_to([P, HG // 2, TT, P])
                for hf in range(2):
                    pool.wait_ge(acs_in[hf], g * 16 + 16)
                    blocks = acs_b[:, hf].rearrange("p h (t l) -> p h t l", l=P)
                    nc.gpsimd.tensor_tensor(blocks, blocks, mask, ALU.add).then_inc(acs_masked, 1)
                by_head = "p (h d) -> p h d"
                pool.wait_ge(xrow_ready, g + 1)
                for t in range(TT):
                    x_heads = y_row[:, t].rearrange(by_head, d=HP)
                    last = nc.gpsimd.tensor_tensor(
                        x_heads, x_heads, d_skip_b[:, bass.ds(g * HG, HG)].unsqueeze(2).broadcast_to([P, HG, HP]), ALU.mult)
                last.then_inc(skip_ready, 1)

            pool.wait_ge(acs_ready, 2)
            pool.dma_start(acs_dram[:], acsT[:]).then_inc(acs_out, 16)
            pool.wait_ge(acs_out, 16)
            loads(0)
            group(0)
            with repeat(pool, G - 1, [(own, 2)]) as i:
                pool.wait_ge(decay_exp, i * 2 + 2)
                loads(i + 1)
                tail(i)
                group(i + 1)
            tail(G - 1)
            pool.wait_ge(x2_ss, TT)
            rsqrt(x2_scale, D, x2_sums, x2_scratch, NORM_EPS).then_inc(x2_rstd, 1)

        @block.tensor
        def _(pe):
            unit, pair = Tally(), Tally()

            def rows_unit(p, k0, stat_hi, stat_lo, first, last):
                r = unit.n % RING
                pe.wait_ge(lo_ready, unit.step())
                for kk in range(UK):
                    for t in range(TT):
                        cut = slice(t * P, (t + 1) * P)
                        for n, (a, w) in enumerate(((stat_hi, w_hi), (stat_hi, w_lo), (stat_lo, w_hi))):
                            done = nc.tensor.matmul(acc[p][:, t], a[:, k0 + kk, cut], w[:, r, kk], start=first and kk == n == 0,
                                                    stop=last and kk == UK - 1 and n == 2)
                done.then_inc(mm_done, 1)

            def cols_unit(p, k0, mov_hi, mov_lo, first, last):
                r = unit.n % RING
                pe.wait_ge(lo_ready, unit.step())
                for kk in range(UK):
                    for c in range(CT):
                        out_at = acc[p][:, c // 2, (c % 2) * T:(c % 2 + 1) * T]
                        cut = slice(c * P, (c + 1) * P)
                        for n, (w, a) in enumerate(((w_hi, mov_hi), (w_hi, mov_lo), (w_lo, mov_hi))):
                            done = nc.tensor.matmul(out_at, w[:, r, kk, cut], a[:, k0 + kk], start=first and kk == n == 0 and c % 2 == 0,
                                                    stop=last and kk == UK - 1 and n == 2, skip_group_check=True)
                done.then_inc(mm_done, 1)

            def chunk(kind, p, hi, lo, units=UPC, between=None):
                pe.wait_ge(acc_free[p], pair.now(1))
                for u in range(units):
                    kind(p, u * UK, hi, lo, u == 0, u == units - 1)
                    if between is not None:
                        between(u)
                if p:
                    pair.step()

            def transpose(out_at, in_):
                return nc.tensor.transpose(out_at, in_, ident)

            def keep_warm(times):
                for _ in range(times):
                    nc.tensor.matmul(acc[1][:, 1, 0:P], ones[:], ones[:], start=True, stop=True)

            pe.wait_ge(ones_ready, 1)
            keep_warm(WARM_START)
            pe.wait_ge(const_in, 16)
            pe.wait_ge(rows_in, 7 * 16)
            nc.tensor.transpose(acc[1][:, 0, 0:R_CONV], rows[0:R_CONV, 0], ident[0:R_CONV, 0:R_CONV])
            nc.tensor.transpose(acc[1][:, 0, R_CONV:2 * R_CONV], rows[0:R_CONV, 1], ident[0:R_CONV, 0:R_CONV])
            nc.tensor.transpose(acc[1][:, 0, 2 * R_CONV:2 * R_CONV + R_ALL], rows[0:R_ALL, 2],
                                ident[0:R_ALL, 0:R_ALL]).then_inc(rows_T, 1)

            def h_columns(b, t):
                for k in (2 * b, 2 * b + 1):
                    at_col = (k % 2) * T + t * P
                    last = transpose(side[:, b % 4, at_col:at_col + P], x_row[:, t, k * P:(k + 1) * P])
                return last

            for t in range(TT):
                if t:
                    keep_warm(WARM_TILE)
                pe.wait_ge(x_normed, t + 1)
                for b in range(4):
                    last = h_columns(b, t)
                    if t == TT - 1:
                        last.then_inc(side_T, 1)
            pe.wait_ge(x_normed, TT + 1)

            def h_between(u):
                if u + 1 < UPC:
                    pe.wait_ge(side_lo, u + 2)
                if u + 4 < KD // 2:
                    h_columns(u + 4, 0)
                    h_columns(u + 4, 1).then_inc(side_T, 1)

            keep_warm(WARM_UNIT)
            pe.wait_ge(side_lo, 1)
            chunk(rows_unit, 0, h_hi, h_lo, between=h_between)
            pe.wait_ge(cols_ready, 2)
            chunk(rows_unit, 1, h_hi, h_lo)
            with repeat(pe, 5, [(unit, 2 * UPC), (pair, 1)]) as i:
                for c in range(2):
                    chunk(rows_unit, c, h_hi, h_lo)

            def head_rows(h, b):
                for w in range(2):
                    for t in range(TT):
                        n = w * TT + t
                        last = transpose(side[:, 0, n * P:(n + 1) * P], qk_row[:, b, w, t])
                last.then_inc(qk_T, 1)

            def head_scores(h):
                pe.wait_ge(qkT_ready, h + 1)
                pe.wait_ge(prob_ready, h + STARTED)
                for m in range(2):
                    half = slice(m * DH, (m + 1) * DH)
                    for q in range(TT):
                        first, width = q * P, (q + 1) * P
                        nc.tensor.matmul(side[:, 1 + m, first:first + width], qkT[half, 0, q * P:(q + 1) * P],
                                         qkT[half, 1, 0:width], start=True, stop=False)
                        last = nc.tensor.matmul(side[:, 1 + m, first + width - P:first + width], ident_b[:], mask_b[:],
                                                start=False, stop=True)
                last.then_inc(scores, 1)

            def head_weights(h):
                pe.wait_ge(wts_ready, h + 1 + STARTED)
                for n in range(3):
                    last = transpose(side[:, 0, n * P:(n + 1) * P], wts[:, n * P:(n + 1) * P])
                last.then_inc(wts_T, 1)

            def head_values(h):
                pe.wait_ge(wtsT_ready, h + 1)
                pe.wait_ge(o_sums, h + STARTED)
                v0, v1 = (v_all[:, t, bass.ds(h * P, P)] for t in range(TT))
                nc.tensor.matmul(side[:, 3, 0:P], wtsT[:, 0:P], v0, start=True, stop=True)
                nc.tensor.matmul(side[:, 3, P:2 * P], wtsT[:, P:2 * P], v0, start=True, stop=False)
                nc.tensor.matmul(side[:, 3, P:2 * P], wtsT[:, 2 * P:3 * P], v1, start=False, stop=True).then_inc(pv, 1)

            def head_out(h, b):
                pe.wait_ge(o_ready, h + 1)
                for t in range(TT):
                    last = transpose(side[:, 0, t * P:(t + 1) * P], o_row[:, b, t])
                last.then_inc(o_T, 1)

            pe.wait_ge(setup_done, 1)

            def heads_between(a):
                def between(u):
                    if u == 0:
                        pe.wait_ge(row_in[0], a * 8 + 16)
                        pe.wait_ge(ya_lo_ready, a + STARTED)
                        head_rows(a, 0)
                    if u == 1:
                        head_scores(a)
                        pe.wait_ge(row_in[1], a * 8 + 16)
                        head_rows(a + 1, 1)
                    if u == 2:
                        head_scores(a + 1)
                    if u == 3:
                        head_weights(a)
                    if u == 4:
                        head_values(a)
                        head_weights(a + 1)
                    if u == 5:
                        head_values(a + 1)
                    if u == 6:
                        head_out(a, 0)
                    if u == 7:
                        pe.wait_ge(ya_lo_ready, a + 1 + STARTED)
                        head_out(a + 1, 1)
                return between

            for n in range(2):
                with repeat(pe, 2, [(unit, 2 * UPC), (pair, 1)]) as i:
                    for c in range(2):
                        chunk(cols_unit, c, h_hi, h_lo, between=heads_between(i * 4 + (8 * n + 2 * c)))
            def dt_products():
                pe.wait_ge(wdt_ready, 1)
                pe.wait_ge(prob_ready, NA + STARTED)
                for k in range(KD):
                    for n, (w, a) in enumerate(((wdt_hi, h_hi), (wdt_hi, h_lo), (wdt_lo, h_hi))):
                        last = nc.tensor.matmul(side[0:HS, 1, 0:T], w[:, k], a[:, k], start=k == n == 0,
                                                stop=k == KD - 1 and n == 2)
                last.then_inc(dtT_sum, 1)
                pe.wait_ge(dtT_ready, 1)
                for t in range(TT):
                    last = nc.tensor.transpose(side[:, 2, t * HS:(t + 1) * HS], dtT[:, t * P:(t + 1) * P], ident[0:HS, 0:HS])
                last.then_inc(dt_sum, 1)

            def cumulative():
                pe.wait_ge(dA_ready, 1)
                nc.tensor.matmul(side[:, 1, 0:HS], tri, dA[:, 0], start=True, stop=True)
                nc.tensor.matmul(side[:, 1, HS:2 * HS], ones[:], dA[:, 0], start=True, stop=False)
                nc.tensor.matmul(side[:, 1, HS:2 * HS], tri, dA[:, 1], start=False, stop=True)
                pe.wait_ge(after_ready, 1)
                nc.tensor.matmul(side[:, 3, 0:HS], after[:], dA[:, 0], start=True, stop=True)
                nc.tensor.matmul(side[:, 3, HS:2 * HS], tri, dA[:, 1], start=True, stop=True)
                nc.tensor.matmul(side[0:HS, 2, 0:P], dA[:, 0], tri, start=True, stop=True)
                nc.tensor.matmul(side[0:HS, 2, P:T], dA[:, 0], ones[:], start=True, stop=False)
                nc.tensor.matmul(side[0:HS, 2, P:T], dA[:, 1], tri, start=False, stop=True).then_inc(acs_sum, 1)

            def last_heads(u):
                if u == UPC - 2:
                    pe.wait_ge(ya_lo_ready, NA + STARTED)

            dt_products()
            pe.wait_ge(ya_lo_ready, NA - UK + STARTED)
            with repeat(pe, 2, [(unit, 2 * UPC), (pair, 1)]) as i:
                for c in range(2):
                    chunk(cols_unit, c, ya_hi, ya_lo, between=last_heads)

            cumulative()

            def y_products(g, hf):
                if hf == 0:
                    pe.wait_ge(decay_ready, g * 2 + 2)
                    pe.wait_ge(xdt_ready, g + 1)
                    pe.wait_ge(cb_ready, g + 1)
                for h in range(hf * 4, hf * 4 + 4):
                    cut = slice(h * HP, (h + 1) * HP)
                    for t in range(TT):
                        nc.tensor.matmul(side[:, t, cut], decay[:, h, t], xdt[:, t, cut], start=True, stop=True)
                if hf:
                    pe.wait_ge(xdt_end_ready, g + 1)
                    pe.wait_ge(xrow_ready, g + 1)
                    nc.tensor.matmul(side[:, 2], cb[:, P:2 * P], xdt_end[:], start=True, stop=True).then_inc(y_sum, 1)

            def to_columns(tile, first):
                for n in range(CT):
                    for t in range(TT):
                        at_col = (n % 2) * T + t * P
                        last = transpose(side[:, 2 + n // 2, at_col:at_col + P], tile[:, t, first + n * P:first + (n + 1) * P])
                return last

            def tail_between(g):
                def between(u):
                    if u in (2, 3):
                        y_products(g, u - 2)
                return between

            def y_columns(g):
                pe.wait_ge(y_ready, g + 1)
                pe.wait_ge(xrow_ready, g + 1)
                to_columns(y_row, 0).then_inc(y_T, 1)

            def z_between(g, first=False):
                def between(u):
                    if u == 0:
                        pe.wait_ge(bT_ready, g + 1)
                        if first:
                            pe.wait_ge(acs_ready, 2)
                        else:
                            pe.wait_ge(y_added, g)
                        c_rows = bc[:, bass.ds(g + G, 1)].rearrange("p o t -> p (o t)")
                        c_late = bc[:, bass.ds(g + G, 1), P:T].rearrange("p o t -> p (o t)")
                        nc.tensor.matmul(side[:, 0, 0:T], bT[:, 0:P], c_rows, start=True, stop=True)
                        nc.tensor.matmul(side[:, 0, T:T + P], bT[:, P:T], c_late, start=True, stop=True).then_inc(cb_sum, 1)
                        if not first:
                            y_columns(g - 1)
                    if u == 3:
                        pe.wait_ge(xs_ready, g + 1)
                        if not first:
                            pe.wait_ge(yT_ready, g)
                        for n in range(CT):
                            for t in range(TT):
                                last = transpose(side[:, 2 + t, n * P:(n + 1) * P], conv_x[:, n, t * P:(t + 1) * P])
                        last.then_inc(xs_T, 1)
                return between

            chunk(cols_unit, 0, h_hi, h_lo)
            chunk(rows_unit, 1, h_hi, h_lo, between=z_between(0, True))
            with repeat(pe, G - 1, [(unit, 2 * UPC), (pair, 1)]) as i:
                chunk(cols_unit, 0, h_hi, h_lo, between=tail_between(i))
                chunk(rows_unit, 1, h_hi, h_lo, between=z_between(i + 1))
            def last_columns(u):
                if u == 0:
                    y_columns(G - 1)

            for c, between in enumerate((tail_between(G - 1), last_columns, None, None)):
                chunk(cols_unit, c % 2, h_hi, h_lo, between=between)
            pe.wait_ge(y_lo_ready, KI // 4)
            with repeat(pe, 2, [(unit, 4 * UPC), (pair, 1)]) as i:
                for c in range(2):
                    chunk(cols_unit, c, y_hi, y_lo, 2 * UPC)

            def residual_columns(c):
                pe.wait_ge(x2_ready, c + 1)
                if c:
                    pe.wait_ge(x2_lo_ready, c)
                else:
                    pe.wait_ge(yT_ready, G)
                to_columns(x2, c * CW).then_inc(x2_T, 1)

            def out_between(c):
                def between(u):
                    if c == 0 and u == UPC - 3:
                        pe.wait_ge(m_lo_ready, 4)
                    if c and u == 3:
                        residual_columns(c - 1)
                return between

            pe.wait_ge(m_lo_ready, 3)
            for c in range(D // CW):
                chunk(rows_unit, c % 2, m_hi, m_lo, between=out_between(c))

            def first_ffn(u):
                if u == 1:
                    residual_columns(3)
                if u == UPC - 3:
                    pe.wait_ge(x2_lo_ready, 4)
                if u == 7:
                    pe.wait_ge(diag_ready, 1)
                    for t in range(TT):
                        last = nc.tensor.matmul(side[:, 0, t * P:(t + 1) * P], ones[:], diag[:, t], start=True, stop=True)
                    last.then_inc(rstd_T, 1)

            pe.wait_ge(x2_lo_ready, 3)
            chunk(cols_unit, 0, x2T_hi, x2T_lo, between=first_ffn)
            chunk(cols_unit, 1, x2T_hi, x2T_lo)
            with repeat(pe, FF // CW - 1, [(unit, 2 * UPC), (pair, 1)]) as i:
                for c in range(2):
                    chunk(cols_unit, c, x2T_hi, x2T_lo)

            def last_ffn(u):
                if u == KF // UK - 3:
                    pe.wait_ge(a_lo_ready, FF // CW)

            pe.wait_ge(a_lo_ready, FF // CW - 1)
            with repeat(pe, 2, [(unit, KF), (pair, 1)]) as i:
                for c in range(2):
                    chunk(rows_unit, c, a_hi, a_lo, KF // UK, between=last_ffn)


def kernel(**inputs):
    import concourse.bacc as bacc
    from concourse.bass_utils import run_bass_kernel_spmd

    nc = bacc.Bacc("TRN2", target_bir_lowering=False, num_devices=1)
    names = ("x", "mix_norm_w", "w_in", "conv_w", "conv_b", "dt_bias", "a_log", "d_skip", "ssm_norm_w", "w_ssm_proj",
             "q_norm_w", "k_norm_w", "lambda_q1", "lambda_k1", "lambda_q2", "lambda_k2", "subln_w", "w_attn_proj",
             "w_out", "ffn_norm_w", "w_ffn_gate", "w_ffn_up", "w_ffn_down")
    arrays = {f"in_{n}": np.ascontiguousarray(inputs[n]) for n in names}
    arrays["in_consts"] = constants()
    aps = [nc.dram_tensor(n, a.shape, F32, kind="ExternalInput").ap() for n, a in arrays.items()]
    out = nc.dram_tensor("out", (1, T, D), F32, kind="ExternalOutput").ap()
    layer(nc, *aps, out)
    result = run_bass_kernel_spmd(nc, [arrays], core_ids=[0])
    return result.results[0]["out"]
```
